# Optimizing a Trainium2 kernel written in Bass

```python
import math
import jax
import jax.numpy as jnp
from jax import lax
import numpy as np

D_MODEL = 1024
BATCH = 1
SEQ = 1024
DEPTH = 1

MEM_LEN = 256
NORM_EPS = 1e-5
D_FF = 2816

SSD_WIDTH = D_MODEL // 2
DIFF_WIDTH = D_MODEL - SSD_WIDTH

SSD_HEAD_DIM = 64
SSD_HEADS = SSD_WIDTH // SSD_HEAD_DIM
SSD_GROUPS = 2
SSD_STATE = 128
SSD_CONV = 5
SSD_CHUNK = 128
SSD_CONV_DIM = SSD_WIDTH + 2 * SSD_GROUPS * SSD_STATE

DIFF_HEADS = 4
DIFF_HEAD_DIM = DIFF_WIDTH // (2 * DIFF_HEADS)
DIFF_V_DIM = 2 * DIFF_HEAD_DIM
ROPE_THETA = 500000.0
ROPE_DIM = DIFF_HEAD_DIM // 4
Q_BLOCK = 128

XATTN_HEADS = 4
XATTN_HEAD_DIM = D_MODEL // XATTN_HEADS

IN_SSD = SSD_WIDTH + SSD_CONV_DIM + 2 * SSD_HEADS
IN_DIFF = 3 * DIFF_WIDTH
D_IN_PROJ = IN_SSD + IN_DIFF

kernel_name = "hybrid_ssd_diffattn_macaron_encoder"

def rms_norm(x, g):
    xf = x.astype(jnp.float32)
    y = xf * lax.rsqrt(jnp.mean(xf * xf, axis=-1, keepdims=True) + NORM_EPS)
    return (y * g.astype(jnp.float32)).astype(x.dtype)

def swiglu(h, w_gate, w_up, w_down):
    return (jax.nn.silu(h @ w_gate) * (h @ w_up)) @ w_down

def rope_tables(seq_len):
    pos = jnp.arange(seq_len, dtype=jnp.float32)
    inv_freq = 1.0 / (ROPE_THETA ** (jnp.arange(0, ROPE_DIM, 2, dtype=jnp.float32) / ROPE_DIM))
    ang = pos[:, None] * inv_freq[None, :]
    return jnp.cos(ang), jnp.sin(ang)

def partial_rope(t, cos, sin):
    half = ROPE_DIM // 2
    c = cos[None, :, None, None, :]
    s_ = sin[None, :, None, None, :]
    tf = t[..., :ROPE_DIM].astype(jnp.float32)
    t1, t2 = tf[..., :half], tf[..., half:]
    rot = jnp.concatenate([t1 * c - t2 * s_, t2 * c + t1 * s_], axis=-1).astype(t.dtype)
    return jnp.concatenate([rot, t[..., ROPE_DIM:]], axis=-1)

def segment_decay(a_cum):
    L = a_cum.shape[2]
    diff = a_cum[:, :, :, None] - a_cum[:, :, None, :]
    mask = jnp.tril(jnp.ones((L, L), dtype=bool))[None, None, :, :, None, None]
    return jnp.exp(jnp.where(mask, diff, -jnp.inf))

def ssd_chunked(xh, dt, A, Bg, Cg):
    b, s, h, p = xh.shape
    g, n = Bg.shape[-2], Bg.shape[-1]
    r = h // g
    L = SSD_CHUNK
    c = s // L
    a = (dt * A).reshape(b, c, L, g, r)
    xdt = (xh.astype(jnp.float32) * dt[..., None]).reshape(b, c, L, g, r, p)
    Bc = Bg.astype(jnp.float32).reshape(b, c, L, g, n)
    Cc = Cg.astype(jnp.float32).reshape(b, c, L, g, n)
    a_cum = jnp.cumsum(a, axis=2)
    cb = jnp.einsum("bclgn,bcsgn->bclsg", Cc, Bc)
    y_diag = jnp.einsum("bclsg,bclsgr,bcsgrp->bclgrp", cb, segment_decay(a_cum), xdt)
    decay_to_end = jnp.exp(a_cum[:, :, -1:] - a_cum)
    states = jnp.einsum("bclgn,bclgr,bclgrp->bcgrpn", Bc, decay_to_end, xdt)
    chunk_decay = jnp.exp(a_cum[:, :, -1])

    def step(carry, inp):
        st, dec = inp
        return carry * dec[..., None, None] + st, carry

    _, prev = lax.scan(step, jnp.zeros_like(states[:, 0]),
                       (jnp.moveaxis(states, 1, 0), jnp.moveaxis(chunk_decay, 1, 0)))
    prev = jnp.moveaxis(prev, 0, 1)
    y_off = jnp.einsum("bclgn,bcgrpn,bclgr->bclgrp", Cc, prev, jnp.exp(a_cum))
    return (y_diag + y_off).reshape(b, s, h, p)

def ssd_mixer(zxbcdt, conv_w, conv_b, dt_bias_fwd, dt_bias_bwd, A_log_fwd, A_log_bwd, D_skip, norm_g):
    b, s, _ = zxbcdt.shape
    z = zxbcdt[..., :SSD_WIDTH]
    xbc = zxbcdt[..., SSD_WIDTH:SSD_WIDTH + SSD_CONV_DIM]
    dt_raw = zxbcdt[..., SSD_WIDTH + SSD_CONV_DIM:].astype(jnp.float32)
    xbc = lax.conv_general_dilated(
        xbc, conv_w[:, None, :], window_strides=(1,),
        padding=[(SSD_CONV // 2, SSD_CONV // 2)],
        dimension_numbers=("NWC", "WIO", "NWC"),
        feature_group_count=SSD_CONV_DIM) + conv_b
    xbc = jax.nn.silu(xbc)
    xs = xbc[..., :SSD_WIDTH].reshape(b, s, SSD_HEADS, SSD_HEAD_DIM)
    Bg = xbc[..., SSD_WIDTH:SSD_WIDTH + SSD_GROUPS * SSD_STATE].reshape(b, s, SSD_GROUPS, SSD_STATE)
    Cg = xbc[..., SSD_WIDTH + SSD_GROUPS * SSD_STATE:].reshape(b, s, SSD_GROUPS, SSD_STATE)
    dt_f = jax.nn.softplus(dt_raw[..., :SSD_HEADS] + dt_bias_fwd.astype(jnp.float32))
    dt_b = jax.nn.softplus(dt_raw[..., SSD_HEADS:] + dt_bias_bwd.astype(jnp.float32))
    A_f = -jnp.exp(A_log_fwd.astype(jnp.float32))
    A_b = -jnp.exp(A_log_bwd.astype(jnp.float32))
    flip = lambda t: jnp.flip(t, axis=1)
    y_f = ssd_chunked(xs, dt_f, A_f, Bg, Cg)
    y_b = flip(ssd_chunked(flip(xs), flip(dt_b), A_b, flip(Bg), flip(Cg)))
    y = y_f + y_b + D_skip.astype(jnp.float32)[:, None] * xs.astype(jnp.float32)
    y = y.reshape(b, s, SSD_WIDTH) * jax.nn.silu(z.astype(jnp.float32))
    y = rms_norm(y.reshape(b, s, SSD_GROUPS, SSD_WIDTH // SSD_GROUPS),
                 norm_g.reshape(SSD_GROUPS, SSD_WIDTH // SSD_GROUPS))
    return y.reshape(b, s, SSD_WIDTH).astype(zxbcdt.dtype)

def diff_attention(qkv, lambda_q1, lambda_k1, lambda_q2, lambda_k2, subln_g, lambda_init):
    b, s, _ = qkv.shape
    H, d = DIFF_HEADS, DIFF_HEAD_DIM
    q = qkv[..., :DIFF_WIDTH].reshape(b, s, H, 2, d)
    k = qkv[..., DIFF_WIDTH:2 * DIFF_WIDTH].reshape(b, s, H, 2, d)
    v = qkv[..., 2 * DIFF_WIDTH:].reshape(b, s, H, DIFF_V_DIM)
    cos, sin = rope_tables(s)
    q = partial_rope(q, cos, sin) * (d ** -0.5)
    k = partial_rope(k, cos, sin)
    f32 = jnp.float32
    lam = (jnp.exp(jnp.sum(lambda_q1.astype(f32) * lambda_k1.astype(f32)))
           - jnp.exp(jnp.sum(lambda_q2.astype(f32) * lambda_k2.astype(f32))) + lambda_init)
    qb = jnp.moveaxis(q.reshape(b, s // Q_BLOCK, Q_BLOCK, H, 2, d), 1, 0)

    def block(q_blk):
        sc = jnp.einsum("bqhtd,bkhtd->bhtqk", q_blk, k).astype(f32)
        pr = jax.nn.softmax(sc, axis=-1)
        a = pr[:, :, 0] - lam * pr[:, :, 1]
        return jnp.einsum("bhqk,bkhe->bqhe", a, v.astype(f32)).astype(v.dtype)

    o = lax.map(block, qb)
    o = jnp.moveaxis(o, 0, 1).reshape(b, s, H, DIFF_V_DIM)
    o = rms_norm(o, subln_g) * (1.0 - lambda_init)
    return o.reshape(b, s, DIFF_WIDTH).astype(qkv.dtype)

def memory_cross_attention(h, mem_h, w_q, w_kv, w_o):
    b, s, _ = h.shape
    m = mem_h.shape[1]
    q = (h @ w_q).reshape(b, s, XATTN_HEADS, XATTN_HEAD_DIM)
    kv = (mem_h @ w_kv).reshape(b, m, 2, XATTN_HEADS, XATTN_HEAD_DIM)
    k, v = kv[:, :, 0], kv[:, :, 1]
    sc = jnp.einsum("bqhd,bkhd->bhqk", q, k).astype(jnp.float32) * (XATTN_HEAD_DIM ** -0.5)
    pr = jax.nn.softmax(sc, axis=-1)
    o = jnp.einsum("bhqk,bkhd->bqhd", pr, v.astype(jnp.float32)).astype(h.dtype)
    return o.reshape(b, s, D_MODEL) @ w_o

def setup_inputs(seed: int = 0) -> dict:
    key = jax.random.key(seed)
    keys = iter(jax.random.split(key, 40))
    f32 = jnp.float32

    def normal(shape, scale):
        return jax.random.normal(next(keys), shape, dtype=f32) * scale

    def gain(shape):
        return 1.0 + normal(shape, 0.02)

    x = normal((BATCH, SEQ, D_MODEL), 1.0)
    mem = normal((BATCH, MEM_LEN, D_MODEL), 1.0)
    dt0_f = jnp.exp(jax.random.uniform(next(keys), (DEPTH, SSD_HEADS), minval=math.log(1e-3), maxval=math.log(1e-1)))
    dt0_b = jnp.exp(jax.random.uniform(next(keys), (DEPTH, SSD_HEADS), minval=math.log(1e-3), maxval=math.log(1e-1)))
    return {
        "x": x,
        "mem": mem,
        "ffn1_norm_g": gain((DEPTH, D_MODEL)),
        "ffn1_w_gate": normal((DEPTH, D_MODEL, D_FF), D_MODEL ** -0.5),
        "ffn1_w_up": normal((DEPTH, D_MODEL, D_FF), D_MODEL ** -0.5),
        "ffn1_w_down": normal((DEPTH, D_FF, D_MODEL), D_FF ** -0.5),
        "mix_norm_g": gain((DEPTH, D_MODEL)),
        "w_in": normal((DEPTH, D_MODEL, D_IN_PROJ), D_MODEL ** -0.5),
        "conv_w": normal((DEPTH, SSD_CONV, SSD_CONV_DIM), SSD_CONV ** -0.5),
        "conv_b": normal((DEPTH, SSD_CONV_DIM), 0.01),
        "dt_bias_fwd": dt0_f + jnp.log(-jnp.expm1(-dt0_f)),
        "dt_bias_bwd": dt0_b + jnp.log(-jnp.expm1(-dt0_b)),
        "A_log_fwd": jnp.log(jax.random.uniform(next(keys), (DEPTH, SSD_HEADS), minval=1.0, maxval=16.0)),
        "A_log_bwd": jnp.log(jax.random.uniform(next(keys), (DEPTH, SSD_HEADS), minval=1.0, maxval=16.0)),
        "D_skip": 1.0 + normal((DEPTH, SSD_HEADS), 0.1),
        "ssd_norm_g": gain((DEPTH, SSD_WIDTH)),
        "lambda_q1": normal((DEPTH, DIFF_HEAD_DIM), 0.1),
        "lambda_k1": normal((DEPTH, DIFF_HEAD_DIM), 0.1),
        "lambda_q2": normal((DEPTH, DIFF_HEAD_DIM), 0.1),
        "lambda_k2": normal((DEPTH, DIFF_HEAD_DIM), 0.1),
        "diff_subln_g": gain((DEPTH, DIFF_V_DIM)),
        "w_out": normal((DEPTH, D_MODEL, D_MODEL), D_MODEL ** -0.5),
        "xattn_norm_g": gain((DEPTH, D_MODEL)),
        "mem_norm_g": gain((DEPTH, D_MODEL)),
        "xattn_w_q": normal((DEPTH, D_MODEL, D_MODEL), D_MODEL ** -0.5),
        "xattn_w_kv": normal((DEPTH, D_MODEL, 2 * D_MODEL), D_MODEL ** -0.5),
        "xattn_w_o": normal((DEPTH, D_MODEL, D_MODEL), D_MODEL ** -0.5),
        "ffn2_norm_g": gain((DEPTH, D_MODEL)),
        "ffn2_w_gate": normal((DEPTH, D_MODEL, D_FF), D_MODEL ** -0.5),
        "ffn2_w_up": normal((DEPTH, D_MODEL, D_FF), D_MODEL ** -0.5),
        "ffn2_w_down": normal((DEPTH, D_FF, D_MODEL), D_FF ** -0.5),
        "final_norm_g": gain((D_MODEL,)),
    }

def reference(x, mem, ffn1_norm_g, ffn1_w_gate, ffn1_w_up, ffn1_w_down, mix_norm_g, w_in,
              conv_w, conv_b, dt_bias_fwd, dt_bias_bwd, A_log_fwd, A_log_bwd, D_skip, ssd_norm_g,
              lambda_q1, lambda_k1, lambda_q2, lambda_k2, diff_subln_g, w_out,
              xattn_norm_g, mem_norm_g, xattn_w_q, xattn_w_kv, xattn_w_o,
              ffn2_norm_g, ffn2_w_gate, ffn2_w_up, ffn2_w_down, final_norm_g):
    for layer in range(DEPTH):
        lambda_init = 0.8 - 0.6 * math.exp(-0.3 * layer)
        h = rms_norm(x, ffn1_norm_g[layer])
        x = x + 0.5 * swiglu(h, ffn1_w_gate[layer], ffn1_w_up[layer], ffn1_w_down[layer])
        h = rms_norm(x, mix_norm_g[layer])
        proj = h @ w_in[layer]
        y_ssd = ssd_mixer(proj[..., :IN_SSD], conv_w[layer], conv_b[layer],
                          dt_bias_fwd[layer], dt_bias_bwd[layer], A_log_fwd[layer], A_log_bwd[layer],
                          D_skip[layer], ssd_norm_g[layer])
        y_diff = diff_attention(proj[..., IN_SSD:], lambda_q1[layer], lambda_k1[layer],
                                lambda_q2[layer], lambda_k2[layer], diff_subln_g[layer], lambda_init)
        y_mix = jnp.concatenate([y_ssd.astype(x.dtype), y_diff.astype(x.dtype)], axis=-1)
        x = x + y_mix @ w_out[layer]
        h = rms_norm(x, xattn_norm_g[layer])
        m = rms_norm(mem, mem_norm_g[layer])
        x = x + memory_cross_attention(h, m, xattn_w_q[layer], xattn_w_kv[layer], xattn_w_o[layer])
        h = rms_norm(x, ffn2_norm_g[layer])
        x = x + 0.5 * swiglu(h, ffn2_w_gate[layer], ffn2_w_up[layer], ffn2_w_down[layer])
    return rms_norm(x, final_norm_g)


_drawn_inputs = setup_inputs


def setup_inputs(seed=0):
    import zlib

    import numpy as np

    out = dict(_drawn_inputs(seed))
    spreads = {}
    factors = {'ffn1_norm_g': 5.318,
     'conv_b': 6.897,
     'ssd_norm_g': 5.558,
     'diff_subln_g': 6.975,
     'xattn_norm_g': 8.0,
     'mem_norm_g': 8.0,
     'ffn2_norm_g': 8.0,
     'final_norm_g': 2.898}
    for name, (base, spread) in spreads.items():
        noise = np.random.default_rng([zlib.crc32(name.encode()), seed]).standard_normal(out[name].shape)
        drawn = base * np.exp(spread * noise) if base else spread * noise
        out[name] = jnp.asarray(drawn.astype(out[name].dtype))
    for name, factor in factors.items():
        out[name] = (out[name] * factor).astype(out[name].dtype)
    return out
```

```python
from contextlib import ExitStack

import concourse.bass as bass
import numpy as np
from concourse import mybir

F32 = mybir.dt.float32
F32R = mybir.dt.float32r
ACT = mybir.ActivationFunctionType
ALU = mybir.AluOpType
AX = mybir.AxisListType

P = 128
D = 1024
KT = D // P
S = 1024
HALF = 512
TC = S // P
FF = 2816
FC = FF // P
PAIRS = FC // 2
NH = 8
HD = 64
AH = 4
M = 256
LAMBDA_INIT = 0.8 - 0.6
B_XBC, B_Z, B_V, B_QK, B_OUT, B_KV, B_Q, B_O, B_END = 0, 8, 12, 16, 24, 32, 48, 56, 64
EPS = 1e-5
XB = [0, KT * PAIRS, KT * PAIRS + KT, KT * PAIRS + 2 * KT, 2 * KT * PAIRS + 2 * KT]

G_FFN1, G_MIX, G_XQ, G_MEM, G_FFN2, G_FIN = (8 * i for i in range(6))
G_SSD, G_SUB = 48, 52
CONVW, CONVB, DSKIP, DTBIAS, ALOG, LAM = 53, 93, 101, 105, 121, 137
NPAR = LAM + 4 * 64
IDENT, ONES, TRIF, TRIB, ROPEP = (128 * i for i in range(5))
INV1024, INV256, INV128 = 640, 641, 642
NCST = 643


class Steps:

    def __init__(self, eng, sem):
        self.eng, self.sem, self.n = eng, sem, 0

    def mark(self, instruction):
        instruction.then_inc(self.sem, 1)
        self.n = self.n + 1

    def wait(self):
        self.eng.wait_ge(self.sem, self.n)

    def done(self, instruction):
        self.mark(instruction)
        self.wait()


def build(nc, xT, memT, par_d, cst_d, rope_d, wgu1, wd1, wgu2, wd2, w_in, w_dt, w_out, w_q, w_kv, w_o, out):
    ctx = ExitStack()
    at = [16512]

    def place(name, shape, dt, offset=None):
        size = int(np.prod(shape[1:])) * 4
        if offset is None:
            offset = at[0]
            at[0] += -(-size // 32) * 32
        return nc.alloc_sbuf_tensor_at(name, shape, dt, offset=offset), offset

    X, _ = place("X", [P, KT, S], F32)
    XH, XH0 = place("XH", [P, KT, S], F32R)
    XL, XL0 = place("XL", [P, KT, S], F32R)
    RB, _ = place("RB", [P, S], F32)
    par, _ = place("par", [P, NPAR], F32)
    cst, _ = place("cst", [P, NCST], F32)
    rn, _ = place("rn", [P, 3, 16], F32)
    W0 = at[0]

    wgu_raw, o = place("wgu_raw", [P, 2, KT, 2, P], F32)
    wgu_h, o_gh = place("wgu_h", [P, KT, 2, P], F32R)
    wgu_l, o_gl = place("wgu_l", [P, KT, 2, P], F32R)
    wd_raw, _ = place("wd_raw", [P, 2, D], F32)
    wd_h, _ = place("wd_h", [P, 2, D], F32R)
    wd_l, _ = place("wd_l", [P, 2, D], F32R)
    hid_h, _ = place("hid_h", [P, 2, S], F32R)
    hid_l, _ = place("hid_l", [P, 2, S], F32R)
    T0 = at[0]
    tg, _ = place("tg", [P, 2, HALF], F32)
    tsl, _ = place("tsl", [P, 2, HALF], F32)
    tu, _ = place("tu", [P, 2, HALF], F32)
    ta, _ = place("ta", [P, 2, HALF], F32)
    assert at[0] <= nc.sbuf_usable_end, at[0]
    sq, _ = place("sq", [P, 2, S], F32, T0)
    ssum, _ = place("ssum", [P, S], F32, T0 + 2 * S * 4)

    wp_raw, _ = place("wp_raw", [P, 2, KT, P], F32, W0)
    wp_h, _ = place("wp_h", [P, 2, KT, P], F32R, o_gh)
    wp_l, _ = place("wp_l", [P, 2, KT, P], F32R, o_gl)
    HOLE = W0 + 8192
    conv_acc, _ = place("conv_acc", [P, 2, S], F32, HOLE)
    rope, _ = place("rope", [P, 2, S], F32, HOLE)
    memX, _ = place("memX", [P, KT, M], F32, HOLE)
    Z0 = o_gl + 8192
    xbc, _ = place("xbc", [P, KT, S], F32, Z0)
    zy, _ = place("zy", [P, 4, S], F32, Z0 + 32768)
    vo, _ = place("vo", [P, 4, S], F32, Z0 + 49152)
    craw, _ = place("craw", [P, S + 8], F32, Z0 + 65536)
    o_small = Z0 + 65536 + 4 * (S + 8)
    small = []
    for name in ("dt_raw", "dt", "da", "cum", "w_state", "dt_tmp"):
        small.append(place(name, [P, TC, 16], F32, o_small)[0])
        o_small += 512
    dt_raw, dt, da, cum, w_state, dt_tmp = small
    w_dtg = dt_tmp
    etot, _ = place("etot", [P, TC, 16], F32, o_small)
    assert o_small + 512 <= nc.sbuf_usable_end, (o_small, nc.sbuf_usable_end)
    H0 = [XH0]

    def inH(name, shape, dt_=F32):
        t, o = place(name, shape, dt_, H0[0])
        H0[0] = o + -(-int(np.prod(shape[1:])) * 4 // 32) * 32
        assert H0[0] <= XH0 + 65536, name
        return t

    stage = inH("stage", [P, 2, KT, P])
    a_c = inH("a_c", [P, 2, 16])
    xs_n = inH("xs_n", [P, 2, NH, HD])
    b_n = inH("b_n", [P, 2, 2, P])
    xdt = inH("xdt", [P, 2, 2, NH, HD])
    xw = inH("xw", [P, NH, HD])
    arg1 = inH("arg1", [P, NH, P])
    arg2 = inH("arg2", [P, NH, P])
    ecum = [inH("ecum0", [P, 2, NH, P]),
            place("ecum1", [P, 2, NH, P], F32, HOLE)[0]]
    cb = inH("cb", [P, 2, 2, P])
    carry = inH("carry", [P, 2, NH * HD])
    pbc = inH("pbc", [P, 2, NH * HD])
    prev_b, _ = place("prev_b", [P, TC, NH * HD], F32, o_gh)
    tmps, _ = place("tmps", [P, 4, P], F32, Z0 + 65536)
    H0[0] = XH0
    q_h, q_l, k_h, k_l = (inH(n, [P, S], F32R) for n in ("q_h", "q_l", "k_h", "k_l"))
    v_c = inH("v_c", [P, S])
    v_h, v_l = (inH(n, [P, KT, P], F32R) for n in ("v_h", "v_l"))
    pr = inH("pr", [P, 2, 2, S])
    att = inH("att", [P, 2, S])
    stat = inH("stat", [P, 2, 8, 2])
    lam = inH("lam", [P, 8])
    lam_t = inH("lam_t", [P, 2, HD])
    aT_h, o_ = place("aT_h", [P, KT, HALF], F32R, Z0)
    aT_l, _ = place("aT_l", [P, KT, HALF], F32R, Z0 + 16384)
    rg, _ = place("rg", [P, 3, 48], F32, Z0 + 65536)
    g_out, _ = place("g_out", [P, 16], F32, Z0 + 65536 + 1024)
    qx, _ = place("qx", [P, KT, S], F32, Z0)
    kv, _ = place("kv", [P, 16, M], F32, Z0 + 32768)
    mem_h, _ = place("mem_h", [P, KT, M], F32R, Z0 + 49152)
    mem_l, _ = place("mem_l", [P, KT, M], F32R, Z0 + 57344)
    RM, _ = place("RM", [P, M], F32, Z0 + 65536 + 2048)
    rm, _ = place("rm", [P, 3, 2], F32, Z0 + 65536 + 3072)
    H0[0] = XH0
    cq_h, cq_l = (inH(n, [P, 2, S], F32R) for n in ("cq_h", "cq_l"))
    ck_h, ck_l = (inH(n, [P, 2, M], F32R) for n in ("ck_h", "ck_l"))
    cv_c = inH("cv_c", [P, 2, M])
    cv_h, cv_l = (inH(n, [P, 2, M], F32R) for n in ("cv_h", "cv_l"))
    cp = inH("cp", [P, 4, M])
    cpT_h, cpT_l = (inH(n, [P, 2, S], F32R) for n in ("cpT_h", "cpT_l"))
    cst_ = inH("cstat", [P, 2, 8])
    gsq, _ = place("gsq", [P, KT, S], F32, Z0)
    sq_m, _ = place("sq_m", [P, 2, S], F32, Z0)
    ssum_m, _ = place("ssum_m", [P, S], F32, Z0 + 8192)
    msq, _ = place("msq", [P, KT, M], F32, XL0 + 16384)

    ident = cst[:, IDENT:IDENT + P]
    ones = cst[:, ONES:ONES + P]
    trif = cst[:, TRIF:TRIF + P]
    trib = cst[:, TRIB:TRIB + P]
    x_spill = nc.dram_tensor("x_spill", (P, KT, S), F32, kind="Internal").ap()

    with ctx:
        PS = ctx.enter_context(nc.psum_tensor("PS", [P, 8, HALF], F32))
        sems = {}

        def sem(name):
            if name not in sems:
                sems[name] = ctx.enter_context(nc.semaphore(name))
            return sems[name]

        s_par, s_cst, s_x, s_wdt, s_rope, s_mem = (sem(n) for n in ("s_par", "s_cst", "s_x", "s_wdt", "s_rope", "s_mem"))
        s_gu = [sem(f"s_gu{i}") for i in range(2)]
        s_wd = [sem(f"s_wd{i}") for i in range(2)]
        s_wp = [sem(f"s_wp{i}") for i in range(2)]
        s_spill, s_out = sem("s_spill"), sem("s_out")
        s_back = [sem(f"s_back{i}") for i in range(4)]
        gu_hi, gu_lo, gu_used, wd_hi, wd_lo = (sem(n) for n in ("gu_hi", "gu_lo", "gu_used", "wd_hi", "wd_lo"))
        unit_done, unit_free, tg_done, silu_done, ta_done = (sem(n) for n in ("unit_done", "unit_free", "tg_done", "silu_done", "ta_done"))
        hid_hi, hid_lo, down_done = (sem(n) for n in ("hid_hi", "hid_lo", "down_done"))
        x_done, x_hi, x_lo = (sem(n) for n in ("x_done", "x_hi", "x_lo"))
        sq_done, sq_added = sem("sq_done"), sem("sq_added")
        rs_done, rs_inv, rn_done, rb_done, r_ready = (sem(n) for n in ("rs_done", "rs_inv", "rn_done", "rb_done", "r_ready"))
        wp_hi, wp_lo, blk_done, blk_free = (sem(n) for n in ("wp_hi", "wp_lo", "blk_done", "blk_free"))
        conv_done, conv_silu, swap_done, qk_ready = (sem(n) for n in ("conv_done", "conv_silu", "swap_done", "qk_ready"))
        wdt_done, dt_done, dt_out = (sem(n) for n in ("wdt_done", "dt_done", "dt_out"))
        sp_step, sp_act, cum_done = (sem(n) for n in ("sp_step", "sp_act", "cum_done"))
        stage_done, nat_tr, nat_done, xw_done, st_done, pb_done = (sem(n) for n in ("stage_done", "nat_tr", "nat_done", "xw_done", "st_done", "pb_done"))
        rows_done, arg_done, e_done, ecum_done, xdt_done, cdec_done = (sem(n) for n in ("rows_done", "arg_done", "e_done", "ecum_done", "xdt_done", "cdec_done"))
        cb_done, cb_used, m_done, y_done, y_out, carry_done = (sem(n) for n in ("cb_done", "cb_used", "m_done", "y_done", "y_out", "carry_done"))
        stage2, nat2_tr, nat2_done, xw2_done, st2_done = (sem(n) for n in ("stage2", "nat2_tr", "nat2_done", "xw2_done", "st2_done"))
        lam_sum, lam_exp = sem("lam_sum"), sem("lam_exp")
        qk_hi, qk_lo, vc_done, v_tr, v_hi, v_lo = (sem(n) for n in ("qk_hi", "qk_lo", "vc_done", "v_tr", "v_hi", "v_lo"))
        sc_done, nm_done, exp_done, comb_done, at_tr, at_hi, at_lo, pv_done, o_done = (sem(n) for n in (
            "sc_done", "nm_done", "exp_done", "comb_done", "at_tr", "at_hi", "at_lo", "pv_done", "o_done"))
        gsq_done, gsum_done, grow_done, ginv_done, groot_done, gs_done, gs_free = (sem(n) for n in (
            "gsq_done", "gsum_done", "grow_done", "ginv_done", "groot_done", "gs_done", "gs_free"))
        g_done = sem("g_done")
        msq_done, msum_done, mrow_done, minv_done, mroot_done, mspread_done, mr_done, mem_hi, mem_lo = (sem(n) for n in (
            "msq_done", "msum_done", "mrow_done", "minv_done", "mroot_done", "mspread_done", "mr_done", "mem_hi", "mem_lo"))
        c_hi, c_lo, cv_copied, cv_tr, cv_hi, cv_lo = (sem(n) for n in ("c_hi", "c_lo", "cv_copied", "cv_tr", "cv_hi", "cv_lo"))
        cs_done, cnm_done, cexp_done, cnorm_done, cp_tr, cp_hi, cp_lo, cpv_done, co_done = (sem(n) for n in (
            "cs_done", "cnm_done", "cexp_done", "cnorm_done", "cp_tr", "cp_hi", "cp_lo", "cpv_done", "co_done"))
        fin_done = sem("fin_done")
        dve_own, pool_own = sem("dve_own"), sem("pool_own")

        block = ctx.enter_context(nc.Block())

        def squares_of(n):
            return (sq_m, ssum_m) if n in (2, 3) else (sq, ssum)

        def chunk(c):
            return bass.ds(c * P, P) if not isinstance(c, int) else slice(c * P, (c + 1) * P)

        def one(j):
            return bass.ds(j, 1)

        @block.sync
        def _(sp):
            sp.dma_start(par[:], par_d).then_inc(s_par, 16)
            sp.dma_start(X[:], xT).then_inc(s_x, 16)
            sp.dma_start(cst[:], cst_d).then_inc(s_cst, 16)

            def ffn_loads(f, wgu, wd):
                c0 = f * FC
                if f:
                    sp.wait_ge(blk_done, B_END)
                for c in range(2):
                    sp.dma_start(wgu_raw[:, c], wgu[c]).then_inc(s_gu[c], 16)
                if f:
                    sp.wait_ge(rs_done, 4)
                for c in range(2):
                    sp.dma_start(wd_raw[:, c], wd[c]).then_inc(s_wd[c], 16)
                with sp.Fori(1, PAIRS) as i:
                    for c in range(2):
                        sp.wait_ge(gu_lo, i * 8 + (4 * (c0 + c - 1)))
                        sp.dma_start(wgu_raw[:, c], wgu[one(i * 2 + c)].rearrange("o p k w n -> (o p) k w n")).then_inc(s_gu[c], 16)
                        sp.wait_ge(wd_lo, i * 2 + (c0 + c - 1))
                        sp.dma_start(wd_raw[:, c], wd[one(i * 2 + c)].rearrange("o p n -> (o p) n")).then_inc(s_wd[c], 16)

            def projection_loads(w, b0, b1):
                with sp.Fori(0, (b1 - b0) // 2) as i:
                    for j in range(2):
                        sp.wait_ge(wp_lo, i * 2 + (b0 + j - 1))
                        sp.dma_start(wp_raw[:, j], w[one(i * 2 + j)].rearrange("o p k n -> (o p) k n")).then_inc(s_wp[j], 16)

            ffn_loads(0, wgu1, wd1)
            sp.dma_start(dt_raw[:], w_dt).then_inc(s_wdt, 16)
            sp.wait_ge(gu_lo, 4 * (FC - 1))
            for j in range(2):
                sp.dma_start(wp_raw[:, j], w_in[j]).then_inc(s_wp[j], 16)
            sp.wait_ge(x_done, XB[1])
            sp.dma_start(x_spill, X[:]).then_inc(s_spill, 16)

            def w_in_loads(i0, i1):
                with sp.Fori(i0, i1) as i:
                    for j in range(2):
                        sp.wait_ge(wp_lo, i * 2 + (j - 1))
                        sp.dma_start(wp_raw[:, j], w_in[one(i * 2 + j)].rearrange("o p k n -> (o p) k n")).then_inc(s_wp[j], 16)

            w_in_loads(1, B_QK // 2)
            sp.wait_ge(conv_silu, B_V)
            sp.dma_start(rope[:], rope_d).then_inc(s_rope, 16)
            w_in_loads(B_QK // 2, B_OUT // 2)

            sp.wait_ge(y_out, TC)
            sp.dma_start(memX[:], memT).then_inc(s_mem, 16)
            sp.wait_ge(pv_done, 2 * AH)
            for q in range(4):
                sp.dma_start(X[:, 2 * q:2 * q + 2], x_spill[:, 2 * q:2 * q + 2]).then_inc(s_back[q], 16)
            projection_loads(w_out, B_OUT, B_KV)
            projection_loads(w_kv, B_KV, B_Q)
            projection_loads(w_q, B_Q, B_O)
            projection_loads(w_o, B_O, B_END)
            ffn_loads(1, wgu2, wd2)
            for k in range(KT):
                sp.wait_ge(fin_done, k + 1)
                sp.dma_start(out[:, k], X[:, k]).then_inc(s_out, 16)
            sp.wait_ge(s_out, 16 * KT)

        @block.scalar
        def _(act):
            def split_weights(i, b, gain, src, hook=None):
                act.wait_ge(s_wp[b % 2], i * 16 + 16 * (b // 2 + 1))
                if hook:
                    hook()
                elif b > 1:
                    act.wait_ge(blk_done, i * 2 + (b - 1))
                elif not isinstance(i, int):
                    act.wait_ge(blk_done, i * 2 + b - 1)
                for k in range(KT):
                    last = nc.scalar.activation(wp_h[:, b % 2, k], wp_raw[:, b % 2, k], ACT.Copy, scale=src[:, gain + k:gain + k + 1])
                last.then_inc(wp_hi, 1)

            def split_x(e, n, x_ready, both=True):
                sq_, _ = squares_of(n)

                def high(k):
                    x_ready(k)
                    nc.scalar.activation(XH[:, k], X[:, k], ACT.Copy).then_inc(x_hi, 1)

                def square(k):
                    if k >= 2 or n > 0:
                        act.wait_ge(sq_added, KT * n + k - 1)
                    nc.scalar.activation(sq_[:, k % 2], X[:, k], ACT.Square).then_inc(sq_done, 1)

                if n == 0:
                    for k in range(KT):
                        high(k)
                    for k in range(KT):
                        square(k)
                else:
                    for k in range(KT):
                        if both:
                            high(k)
                        else:
                            x_ready(k)
                        square(k)

            def root(n):
                act.wait_ge(rs_inv, n + 1)
                nc.scalar.activation(rn[:, 2, 0:TC], rn[:, 1, 0:TC], ACT.Sqrt).then_inc(rn_done, 1)

            def ffn(f, n, gain, before, after):
                c0, u0 = f * FC, 2 * f * FC

                def split_gu(i, c, pieces=range(4), first=False):
                    act.wait_ge(s_gu[c % 2], (i + c // 2) * 16 + 16 * (PAIRS * f + 1))
                    for q in pieces:
                        if not first:
                            if q < 3:
                                act.wait_ge(gu_used, i * 6 + (3 * (c0 + c - 1) + q + 1))
                            else:
                                act.wait_ge(unit_done, i * 4 + 2 * (c0 + c))
                        for k in range(2 * q, 2 * q + 2):
                            last = nc.scalar.activation(wgu_h[:, k], wgu_raw[:, c % 2, k], ACT.Copy,
                                                        scale=par[:, gain + k:gain + k + 1])
                        last.then_inc(gu_hi, 1)

                def split_wd(i, c, first=False):
                    act.wait_ge(s_wd[c], i * 16 + 16 * (PAIRS * f + 1))
                    if not first:
                        act.wait_ge(down_done, i * KT + KT * PAIRS * f)
                    nc.scalar.activation(wd_h[:, c], wd_raw[:, c], ACT.Copy).then_inc(wd_hi, 1)

                def unit(i, u):
                    act.wait_ge(tg_done, i * 4 + (u0 + u + 1))
                    nc.scalar.activation(tsl[:, u % 2], tg[:, u % 2], ACT.Silu).then_inc(silu_done, 1)
                    act.wait_ge(ta_done, i * 4 + (u0 + u + 1))
                    nc.scalar.activation(hid_h[:, u // 2, u % 2 * HALF:(u % 2 + 1) * HALF], ta[:, u % 2],
                                         ACT.Copy).then_inc(hid_hi, 1)

                split_gu(0, 0, first=True)
                before()
                root(n)

                def pair(i, last=False, first=False):
                    unit(i, 0)
                    split_wd(i, 0, first)
                    split_wd(i, 1, first)
                    split_gu(i, 1)
                    unit(i, 1)
                    unit(i, 2)
                    if not last:
                        split_gu(i, 2, range(3))
                    unit(i, 3)
                    if not last:
                        split_gu(i, 2, range(3, 4))

                pair(0, first=f == 0)
                with act.Fori(1, PAIRS - 1) as i:
                    pair(i)
                pair(PAIRS - 1, last=True)
                after()

            def x_loaded(k):
                act.wait_ge(s_x, 16)

            def x_written(n):
                def wait(k):
                    act.wait_ge(x_done, XB[n] - KT + k + 1)
                    if k == 0 and n == 1:
                        act.wait_ge(unit_done, 2 * FC)
                    if k == 0 and n == 3:
                        act.wait_ge(blk_done, B_END)
                return wait

            def to_mixer():
                def ready():
                    act.wait_ge(unit_done, 2 * FC)
                split_weights(0, 0, G_MIX, par, ready)
                split_x(1, 1, x_written(1))
                root(1)

            act.wait_ge(s_par, 16)
            ffn(0, 0, G_FFN1, lambda: split_x(0, 0, x_loaded), to_mixer)

            def conv_block(i, b, dst, j):
                if b < B_Z:
                    act.wait_ge(conv_done, i * 2 + b + 1)
                    nc.scalar.activation(dst[:, one(i * 2 + j)], conv_acc[:, b % 2:b % 2 + 1], ACT.Silu,
                                         bias=par[:, one(i * 2 + (CONVB + j))]).then_inc(conv_silu, 1)
                else:
                    act.wait_ge(blk_free, i * 2 + b + 1)
                    nc.scalar.activation(dst[:, one(i * 2 + j)], conv_acc[:, b % 2:b % 2 + 1], ACT.Silu).then_inc(conv_silu, 1)

            with act.Fori(0, (B_Z - B_XBC) // 2) as i:
                for j in range(2):
                    if j == 0:
                        act.wait_ge(s_wp[1], i * 16 + 16)
                        act.wait_ge(blk_done, i * 2)
                        for k in range(KT):
                            last = nc.scalar.activation(wp_h[:, 1, k], wp_raw[:, 1, k], ACT.Copy, scale=par[:, G_MIX + k:G_MIX + k + 1])
                        last.then_inc(wp_hi, 1)
                    else:
                        split_weights(i, 2, G_MIX, par)
                    conv_block(i, j, xbc, j)
            with act.Fori(0, (B_V - B_Z) // 2) as i:
                for j in range(2):
                    split_weights(i, B_Z + j + 1, G_MIX, par)
                    conv_block(i, B_Z + j, zy, j)
            with act.Fori(0, (B_OUT - 2 - B_V) // 2) as i:
                for j in range(2):
                    split_weights(i, B_V + j + 1, G_MIX, par)
            split_weights(0, B_OUT - 1, G_MIX, par)

            act.wait_ge(sp_step, 1)
            nc.scalar.activation(w_state[:], etot[:], ACT.Exp, scale=-1.0).then_inc(sp_act, 1)
            act.wait_ge(sp_step, 2)
            nc.scalar.activation(cum[:], etot[:], ACT.Ln).then_inc(sp_act, 1)
            act.wait_ge(sp_act, 2)
            nc.scalar.activation(rn[:, 0, :], par[:, ALOG:ALOG + 16], ACT.Exp).then_inc(sp_act, 1)
            act.wait_ge(sp_step, 3)
            nc.scalar.activation(w_state[:], dt_tmp[:], ACT.Exp).then_inc(sp_act, 1)
            nc.scalar.activation(etot[:], PS[:, 6, 0:P].rearrange("p (c h) -> p c h", c=TC), ACT.Exp).then_inc(sp_act, 1)

            def natural(w, p):
                nc.scalar.activation(xs_n[:, p], PS[:, 4].rearrange("p (h d) -> p h d", h=NH), ACT.Copy)
                nc.scalar.activation(b_n[:, p], PS[:, 5, 0:2 * P].rearrange("p (g n) -> p g n", g=2), ACT.Copy).then_inc(w, 1)

            with act.Fori(0, TC - 1) as r:
                act.wait_ge(nat_tr, r + 1)
                act.wait_ge(xw_done, r)
                act.wait_ge(st_done, r)
                natural(nat_done, 0)

            def front(i, c):
                act.wait_ge(nat2_tr, i * 2 + (c + 1))
                if c >= 2 or not isinstance(i, int):
                    act.wait_ge(st2_done, i * 2 + (c - 1))
                    act.wait_ge(xdt_done, i * 2 + (c - 1))
                elif c == 0:
                    act.wait_ge(st_done, TC - 1)
                if c == 0 and isinstance(i, int):
                    act.wait_ge(pb_done, TC)
                else:
                    act.wait_ge(y_done, i * 2 + (c - 1))
                nc.scalar.activation(pbc[:, c % 2:c % 2 + 1], prev_b[:, one(i * 2 + c)], ACT.Copy)
                natural(nat2_done, c % 2)

            def back(i, c):
                act.wait_ge(arg_done, i * 2 + (c + 1))
                nc.scalar.activation(arg1[:], arg1[:], ACT.Exp).then_inc(e_done, 1)
                for d in range(2):
                    last = nc.scalar.activation(ecum[c % 2][:, d], PS[:, 2 * d:2 * d + 2].rearrange("p a (h l) -> p (a h) l", l=P), ACT.Exp)
                last.then_inc(ecum_done, 1)

            front(0, 0)
            with act.Fori(0, TC // 2 - 1) as i:
                for c in range(2):
                    front(i, c + 1)
                    back(i, c)
            front(0, TC - 1)
            back(0, TC - 2)
            back(0, TC - 1)

            act.wait_ge(lam_sum, 1)
            nc.scalar.activation(lam[:, 2:4], lam[:, 0:2], ACT.Exp).then_inc(lam_exp, 1)
            with act.Fori(0, AH) as h:
                act.wait_ge(pv_done, h * 2)
                nc.scalar.activation(q_h[:], X[:, one(h)].rearrange("p o s -> p (o s)"), ACT.Copy).then_inc(qk_hi, 1)
                nc.scalar.activation(k_h[:], X[:, one(h + AH)].rearrange("p o s -> p (o s)"), ACT.Copy).then_inc(qk_hi, 1)
                act.wait_ge(v_tr, h + 1)
                nc.scalar.activation(v_h[:], PS[:, 4:6].rearrange("p a (k e) -> p (a k) e", e=P), ACT.Copy).then_inc(v_hi, 1)
                for s in range(TC + 1):
                    if s < TC:
                        act.wait_ge(comb_done, h * TC + max(s - 1, 0))
                        for t in range(2):
                            act.wait_ge(nm_done, h * 16 + (2 * s + t + 1))
                            nc.scalar.activation(pr[:, s % 2, t], PS[:, 2 * t:2 * t + 2].rearrange("p a b -> p (a b)"), ACT.Exp,
                                                 bias=stat[:, s % 2, 2 + t, 0:1], scale=0.125,
                                                 accum_out=stat[:, s % 2, 4 + t, 0:1]).then_inc(exp_done, 1)
                    if s >= 1:
                        q = s - 1
                        act.wait_ge(at_tr, h * TC + (q + 1))
                        if q % 4 == 0:
                            act.wait_ge(pv_done, h * 2 + q // 4)
                        nc.scalar.activation(aT_h[:, :, q % 4 * P:(q % 4 + 1) * P],
                                             PS[:, 4:6].rearrange("p a (k q) -> p (a k) q", q=P), ACT.Copy).then_inc(at_hi, 1)

            act.wait_ge(pv_done, 2 * AH)
            for k in range(KT):
                if k >= 4:
                    act.wait_ge(o_done, 2 * (k - 3))
                src = zy[:, k] if k < 4 else vo[:, k - 4]
                nc.scalar.activation(gsq[:, k], src, ACT.Square).then_inc(gsq_done, 1)
            act.wait_ge(ginv_done, 1)
            nc.scalar.activation(rg[:, 2], rg[:, 1], ACT.Sqrt).then_inc(groot_done, 1)
            act.wait_ge(g_done, 1)
            split_weights(0, B_OUT, 0, g_out)
            for k in range(KT):
                act.wait_ge(gs_free, k + 1)
                src = zy[:, k] if k < 4 else vo[:, k - 4]
                nc.scalar.activation(XH[:, k], src, ACT.Copy).then_inc(x_hi, 1)
            act.wait_ge(s_mem, 16)
            act.wait_ge(x_lo, 3 * KT)
            nc.scalar.activation(mem_h[:], memX[:], ACT.Copy).then_inc(mem_hi, 1)
            nc.scalar.activation(qx[:, 4:6].rearrange("p a b -> p (a b)"), memX[:].rearrange("p k m -> p (k m)"), ACT.Square).then_inc(msq_done, 1)
            act.wait_ge(minv_done, 1)
            nc.scalar.activation(rm[:, 2], rm[:, 1], ACT.Sqrt).then_inc(mroot_done, 1)

            def square_loop(n, b0, b1, gain, src):
                def square(i, j):
                    act.wait_ge(x_done, i * 2 + (XB[n] - KT + j + 1))
                    act.wait_ge(sq_added, i * 2 + (KT * n + j - 1))
                    nc.scalar.activation(sq_m[:, j:j + 1], X[:, one(i * 2 + j)], ACT.Square).then_inc(sq_done, 1)
                with act.Fori(0, (b1 - b0) // 2 - 1) as i:
                    for j in range(2):
                        split_weights(i, b0 + j + 1, gain, src)
                        square(i, j)
                split_weights(0, b1 - 1, gain, src)
                square(KT // 2 - 1, 0)
                square(KT // 2 - 1, 1)

            square_loop(2, B_OUT, B_KV, 0, g_out)
            split_weights(0, B_KV, G_MEM, par)
            root(2)
            for k in range(KT):
                if k == 0:
                    act.wait_ge(blk_done, B_KV)
                nc.scalar.activation(XH[:, k], X[:, k], ACT.Copy).then_inc(x_hi, 1)
            with act.Fori(0, (B_Q - B_KV) // 2 - 1) as i:
                for j in range(2):
                    split_weights(i, B_KV + j + 1, G_MEM, par)
            split_weights(0, B_Q - 1, G_MEM, par)
            split_weights(0, B_Q, G_XQ, par)
            with act.Fori(0, (B_O - B_Q) // 2 - 1) as i:
                for j in range(2):
                    split_weights(i, B_Q + j + 1, G_XQ, par)
            split_weights(0, B_O - 1, G_XQ, par)

            act.wait_ge(blk_free, B_O - KT)
            with act.Fori(0, AH) as h:
                act.wait_ge(cpv_done, h * 4)
                nc.scalar.activation(cq_h[:], qx[:, bass.ds(h * 2, 2)], ACT.Copy).then_inc(c_hi, 1)
                nc.scalar.activation(ck_h[:], kv[:, bass.ds(h * 2, 2)], ACT.Copy).then_inc(c_hi, 1)
                act.wait_ge(cv_tr, h + 1)
                nc.scalar.activation(cv_h[:], PS[:, 4].rearrange("p (m e) -> p m e", m=2), ACT.Copy).then_inc(cv_hi, 1)
                for s in range(TC + 1):
                    if s < TC:
                        act.wait_ge(cnm_done, h * TC + (s + 1))
                        act.wait_ge(cp_tr, h * TC + max(s - 3, 0))
                        nc.scalar.activation(cp[:, s % 4], PS[:, s % 2, 0:M], ACT.Exp, bias=cst_[:, 0, s:s + 1], scale=0.0625,
                                             accum_out=cst_[:, 1, s:s + 1]).then_inc(cexp_done, 1)
                    if s >= 1:
                        q = s - 1
                        act.wait_ge(cp_tr, h * TC + (q + 1))
                        nc.scalar.activation(cpT_h[:, :, q * P:(q + 1) * P], PS[:, 2 + q % 2, 0:M].rearrange("p (m q) -> p m q", m=2),
                                             ACT.Copy).then_inc(cp_hi, 1)
            split_weights(0, B_O, 8, g_out)
            for k in range(KT):
                if k == 0:
                    act.wait_ge(cpv_done, 4 * AH)
                act.wait_ge(co_done, 4 * (k // 2 + 1))
                nc.scalar.activation(XH[:, k], qx[:, k], ACT.Copy).then_inc(x_hi, 1)
            square_loop(3, B_O, B_END, 8, g_out)

            def to_ffn2():
                for k in range(KT):
                    if k == 0:
                        act.wait_ge(blk_done, B_END)
                        act.wait_ge(x_done, XB[3])
                    nc.scalar.activation(XH[:, k], X[:, k], ACT.Copy).then_inc(x_hi, 1)

            def to_end():
                for k in range(KT):
                    act.wait_ge(x_done, XB[4] - KT + k + 1)
                    act.wait_ge(sq_added, KT * 4 + k - 1)
                    nc.scalar.activation(sq[:, k % 2], X[:, k], ACT.Square).then_inc(sq_done, 1)
                root(4)

            ffn(1, 3, G_FFN2, to_ffn2, to_end)

        @block.gpsimd
        def _(pool):
            own = Steps(pool, pool_own)

            def sum_squares(n):
                sq_, ssum_ = squares_of(n)
                for k in range(KT):
                    pool.wait_ge(sq_done, KT * n + k + 1)
                    if k == 0:
                        if n > 0:
                            pool.wait_ge(rs_done, n)
                        last = nc.gpsimd.tensor_copy(ssum_[:], sq_[:, 0])
                    else:
                        last = nc.gpsimd.tensor_tensor(ssum_[:], ssum_[:], sq_[:, k % 2], ALU.add)
                    last.then_inc(sq_added, 1)
                    pool.wait_ge(sq_added, KT * n + k + 1)

            sum_squares(0)
            sum_squares(1)

            pool.wait_ge(blk_done, B_OUT)
            pool.wait_ge(sp_step, 4)
            with pool.Fori(0, TC - 1) as r:
                c = r * -1 + (TC - 1)
                pool.wait_ge(nat_tr, r)
                pool.tensor_copy(stage[:, 0, 0:6], xbc[:, 0:6, chunk(c)]).then_inc(stage_done, 1)
                pool.wait_ge(nat_done, r + 1)
                pool.wait_ge(st_done, r)
                pool.tensor_tensor(xw[:], xs_n[:, 0], w_state[:, one(c), 8:16].rearrange("p o h -> p (o h)").unsqueeze(2).to_broadcast([P, NH, HD]),
                                   ALU.mult).then_inc(xw_done, 1)

            def front(i, c):
                p = c % 2
                if c >= 2 or not isinstance(i, int):
                    pool.wait_ge(y_out, i * 2 + (c - 1))
                elif c == 0:
                    pool.wait_ge(nat_tr, TC - 1)
                pool.tensor_copy(a_c[:, p:p + 1], da[:, one(i * 2 + c)])
                pool.tensor_copy(stage[:, p], xbc[:, :, chunk(i * 2 + c)]).then_inc(stage2, 1)

            def back(i, c):
                p = c % 2

                def per_head(t, d):
                    return t[:, one(i * 2 + c), 8 * d:8 * d + 8].rearrange("p o h -> p (o h)").unsqueeze(2).to_broadcast([P, NH, HD])
                pool.wait_ge(nat2_done, i * 2 + (c + 1))
                if isinstance(i, int) and c == 0:
                    pool.wait_ge(st_done, TC - 1)
                else:
                    pool.wait_ge(st2_done, i * 2 + c)
                pool.tensor_tensor(xw[:], xs_n[:, p], per_head(w_state, 0), ALU.mult).then_inc(xw2_done, 1)
                for d in range(2):
                    last = pool.tensor_tensor(xdt[:, p, d], xs_n[:, p], per_head(dt, d), ALU.mult)
                last.then_inc(xdt_done, 1)
                pool.wait_ge(ecum_done, i * 2 + (c + 1))
                for d in range(2):
                    e = ecum[p][:, d].rearrange("p (g r) l -> p g r l", g=2)
                    last = pool.tensor_tensor(e, e, stage[:, p, 6:8].unsqueeze(2).to_broadcast([P, 2, 4, P]), ALU.mult)
                last.then_inc(cdec_done, 1)

            front(0, 0)
            with pool.Fori(0, TC // 2 - 1) as i:
                for c in range(2):
                    front(i, c + 1)
                    back(i, c)
            front(0, TC - 1)
            back(0, TC - 2)
            back(0, TC - 1)

            pool.wait_ge(y_out, TC)
            pool.wait_ge(carry_done, TC)
            with pool.Fori(0, AH) as h:
                pool.wait_ge(v_tr, h)
                pool.tensor_copy(v_c[:], vo[:, one(h)].rearrange("p o s -> p (o s)")).then_inc(vc_done, 1)

            for g in range(2):
                pool.wait_ge(gsq_done, 2 * g + 2)
                pool.tensor_tensor(gsq[:, 2 * g], gsq[:, 2 * g], gsq[:, 2 * g + 1], ALU.add).then_inc(gsum_done, 1)
            pool.wait_ge(msq_done, 1)
            own.done(pool.tensor_tensor(qx[:, 4], qx[:, 4], qx[:, 5], ALU.add))
            own.done(pool.tensor_tensor(qx[:, 4, 0:HALF], qx[:, 4, 0:HALF], qx[:, 4, HALF:S], ALU.add))
            pool.tensor_tensor(qx[:, 4, 0:M], qx[:, 4, 0:M], qx[:, 4, M:2 * M], ALU.add).then_inc(msum_done, 1)
            sum_squares(2)
            with pool.Fori(0, AH) as h:
                pool.wait_ge(cv_tr, h)
                pool.wait_ge(blk_free, B_O - KT)
                pool.tensor_copy(cv_c[:], kv[:, bass.ds(h * 2 + 8, 2)]).then_inc(cv_copied, 1)
            sum_squares(3)
            sum_squares(4)

        @block.tensor
        def _(pe):
            def root_rows(n):
                _, ssum_ = squares_of(n)
                pe.wait_ge(sq_added, KT * (n + 1))
                for t in range(TC):
                    last = nc.tensor.matmul(PS[:, 6, t:t + 1], ssum_[:, t * P:(t + 1) * P],
                                            cst[:, INV1024:INV1024 + 1], start=True, stop=True)
                last.then_inc(rs_done, 1)

            def root_spread(n):
                pe.wait_ge(rn_done, n + 1)
                for t in range(TC):
                    last = nc.tensor.matmul(PS[:, 4 + t // 4, t % 4 * P:(t % 4 + 1) * P],
                                            rn[:, 2, t:t + 1].to_broadcast([P, P]), ident, start=True, stop=True)
                last.then_inc(rb_done, 1)

            def ffn(f, n, e):
                c0, u0 = f * FC, 2 * f * FC

                def gate_up(i, c, half, first, firstunit=False):
                    u = 2 * c + half
                    if not first:
                        pe.wait_ge(unit_free, i * 4 + (u0 + u - 1))
                    bank = 2 * half
                    tok = slice(half * HALF, (half + 1) * HALF)
                    for k in range(KT):
                        if half == 0 and k % 2 == 0:
                            pe.wait_ge(gu_lo, i * 8 + (4 * (c0 + c) + k // 2 + 1))
                        if firstunit:
                            pe.wait_ge(x_lo, KT * e + k + 1)
                            if k == KT // 2:
                                root_rows(n)
                        for w in range(2):
                            o = PS[:, bank + w]
                            nc.tensor.matmul(o, wgu_h[:, k, w], XH[:, k, tok], start=k == 0, stop=False)
                            nc.tensor.matmul(o, wgu_h[:, k, w], XL[:, k, tok], start=False, stop=False)
                            last = nc.tensor.matmul(o, wgu_l[:, k, w], XH[:, k, tok], start=False, stop=k == KT - 1)
                        if half == 1 and k in (1, 3, 5):
                            last.then_inc(gu_used, 1)
                    last.then_inc(unit_done, 1)

                def down(i, first):
                    def part(m, c, half):
                        o = PS[:, 4 + 2 * (m % 2) + half]
                        w, tok = slice(m * P, (m + 1) * P), slice(half * HALF, (half + 1) * HALF)
                        nc.tensor.matmul(o, wd_h[:, c, w], hid_h[:, c, tok], start=c == 0, stop=False)
                        nc.tensor.matmul(o, wd_h[:, c, w], hid_l[:, c, tok], start=False, stop=False)
                        return nc.tensor.matmul(o, wd_l[:, c, w], hid_h[:, c, tok], start=False, stop=c == 1)

                    def down_free(i, m):
                        pe.wait_ge(x_done, i * KT + (XB[n] + m - 1))

                    pe.wait_ge(wd_lo, i * 2 + (c0 + 2))
                    pe.wait_ge(hid_lo, i * 4 + (u0 + 2))
                    if first:
                        pe.wait_ge(r_ready, n + 1)
                    for m in range(2):
                        if not first:
                            down_free(i, m)
                        part(m, 0, 0)
                        part(m, 0, 1)
                    pe.wait_ge(hid_lo, i * 4 + (u0 + 3))
                    part(0, 1, 0)
                    part(1, 1, 0)
                    pe.wait_ge(hid_lo, i * 4 + (u0 + 4))
                    part(0, 1, 1).then_inc(down_done, 1)
                    part(1, 1, 1).then_inc(down_done, 1)
                    for m in range(2, KT):
                        down_free(i, m)
                        for c in range(2):
                            for half in range(2):
                                last = part(m, c, half)
                        last.then_inc(down_done, 1)

                def pair(i, first=False):
                    gate_up(i, 0, 0, first, firstunit=first)
                    if first:
                        root_spread(n)
                    gate_up(i, 0, 1, first)
                    gate_up(i, 1, 0, False)
                    gate_up(i, 1, 1, False)
                    down(i, first)

                pair(0, first=True)
                with pe.Fori(1, PAIRS) as i:
                    pair(i)

            def proj(i, b, hi=XH, lo=XL, n_tok=S, free=None, e=None, n=None):
                pe.wait_ge(wp_lo, i * 2 + (b + 1))
                if free:
                    pe.wait_ge(free[0], i * 2 + (b + free[1] - 1))
                w = min(n_tok, HALF)
                for k in range(KT):
                    if e is not None:
                        pe.wait_ge(x_lo, KT * e + k + 1)
                    if n is not None and k == KT // 2:
                        root_rows(n)
                    for half in range(n_tok // w):
                        o, tok = PS[:, 2 * (b % 2) + half, 0:w], slice(half * w, (half + 1) * w)
                        nc.tensor.matmul(o, wp_h[:, b % 2, k], hi[:, k, tok], start=k == 0, stop=False)
                        nc.tensor.matmul(o, wp_h[:, b % 2, k], lo[:, k, tok], start=False, stop=False)
                        last = nc.tensor.matmul(o, wp_l[:, b % 2, k], hi[:, k, tok], start=False, stop=k == KT - 1)
                last.then_inc(blk_done, 1)

            pe.wait_ge(s_cst, 16)
            ffn(0, 0, 0)

            pe.wait_ge(unit_free, 2 * FC)
            proj(0, 0, e=1, n=1)
            root_spread(1)
            proj(0, 1)
            pe.wait_ge(wdt_done, 1)
            for t in range(TC):
                for k in range(KT):
                    last = nc.tensor.matmul(PS[:, 7, 16 * t:16 * t + 16], X[:, k, t * P:(t + 1) * P], w_dtg[:, k], start=k == 0, stop=k == KT - 1)
            last.then_inc(dt_done, 1)
            with pe.Fori(1, B_QK // 2) as i:
                proj(i, 0, free=(blk_free, 0))
                proj(i, 1, free=(blk_free, 0))

            def swap(i, b):
                pe.wait_ge(blk_free, i * 2 + (b + 1))
                pe.wait_ge(qk_ready, i * 2 + (b - B_QK - 1)) if (b - B_QK >= 2 or not isinstance(i, int)) else pe.wait_ge(dt_out, 1)
                for half in range(2):
                    last = nc.tensor.matmul(PS[:, 4 + 2 * (b % 2) + half], cst[:, ROPEP:ROPEP + P],
                                            X[:, one(i * 2 + (b - B_QK)), half * HALF:(half + 1) * HALF].rearrange("p o s -> p (o s)"), start=True, stop=True)
                last.then_inc(swap_done, 1)

            proj(0, B_QK, free=(blk_free, 0))
            proj(0, B_QK + 1, free=(blk_free, 0))
            swap(0, B_QK)
            with pe.Fori(0, 3) as i:
                proj(i, B_QK + 2, free=(blk_free, 0))
                swap(i, B_QK + 1)
                proj(i, B_QK + 3, free=(blk_free, 0))
                swap(i, B_QK + 2)
            swap(0, B_OUT - 1)

            pe.wait_ge(qk_ready, 8)
            pe.wait_ge(dt_out, 2)
            c7 = PS[:, 7, 0:P].rearrange("p (c h) -> p c h", c=TC)
            nc.tensor.matmul(c7[:, :, 0:8], trif, da[:, :, 0:8], start=True, stop=True)
            nc.tensor.matmul(c7[:, :, 8:16], trib, da[:, :, 8:16], start=True, stop=True)
            nc.tensor.matmul(PS[:, 6, 0:P], ones, da[:], start=True, stop=True).then_inc(cum_done, 1)

            def transposes(p, w):
                for k in range(4):
                    nc.tensor.transpose(PS[:, 4, k * P:(k + 1) * P], stage[:, p, k], ident)
                for g in range(2):
                    last = nc.tensor.transpose(PS[:, 5, g * P:(g + 1) * P], stage[:, p, 4 + g], ident)
                last.then_inc(w, 1)

            def states(p, w):
                for g in range(2):
                    last = nc.tensor.matmul(PS[:, 6, 256 * g:256 * g + 256], b_n[:, p, g], xw[:, 4 * g:4 * g + 4].rearrange("p h d -> p (h d)"),
                                            start=True, stop=True)
                last.then_inc(w, 1)

            pe.wait_ge(sp_act, 5)
            with pe.Fori(0, TC - 1) as r:
                pe.wait_ge(stage_done, r + 1)
                pe.wait_ge(nat_done, r)
                transposes(0, nat_tr)
                pe.wait_ge(xw_done, r + 1)
                pe.wait_ge(pb_done, r + 1)
                states(0, st_done)

            def front(i, c):
                p = c % 2
                pe.wait_ge(stage2, i * 2 + (c + 1))
                if c >= 1 or not isinstance(i, int):
                    pe.wait_ge(nat2_done, i * 2 + c)
                    pe.wait_ge(cb_used, i * 2 + c)
                transposes(p, nat2_tr)
                if c >= 1 or not isinstance(i, int):
                    pe.wait_ge(ecum_done, i * 2 + c)
                for d in range(2):
                    for h in range(NH):
                        last = nc.tensor.matmul(PS[:, 2 * d + h // 4, h % 4 * P:(h % 4 + 1) * P],
                                                a_c[:, p, 8 * d + h:8 * d + h + 1].to_broadcast([P, P]), (trif, trib)[d], start=True, stop=True)
                last.then_inc(rows_done, 1)
                pe.wait_ge(nat2_done, i * 2 + (c + 1))
                for g in range(2):
                    last = nc.tensor.matmul(PS[:, 5, 256 + g * P:256 + (g + 1) * P], stage[:, p, 4 + g], stage[:, p, 6 + g], start=True, stop=True)
                last.then_inc(cb_done, 1)

            def back(i, c, first=False):
                p = c % 2
                pe.wait_ge(xw2_done, i * 2 + (c + 1))
                if first:
                    pe.wait_ge(pb_done, TC)
                pe.wait_ge(carry_done, i * 2 + c + 0)
                states(p, st2_done)
                pe.wait_ge(m_done, i * 2 + (c + 1))
                pe.wait_ge(xdt_done, i * 2 + (c + 1))
                pe.wait_ge(cdec_done, i * 2 + (c + 1))
                if not first:
                    pe.wait_ge(y_out, i * 2 + c)
                for h in range(NH):
                    r, col, hc = h % 2 * HD, h // 2 * P, slice(h * HD, (h + 1) * HD)
                    o = PS[r:r + HD, 7, col:col + P]
                    nc.tensor.matmul(o, xdt[:, p, 0, h], arg1[:, h], start=True, stop=False)
                    nc.tensor.matmul(o, xdt[:, p, 1, h], arg2[:, h], start=False, stop=False)
                    nc.tensor.matmul(o, carry[:, p, hc], ecum[p][:, 0, h], start=False, stop=False)
                    last = nc.tensor.matmul(o, pbc[:, p, hc], ecum[p][:, 1, h], start=False, stop=True)
                last.then_inc(y_done, 1)

            front(0, 0)
            with pe.Fori(0, TC // 2 - 1) as i:
                for c in range(2):
                    front(i, c + 1)
                    back(i, c)
            front(0, TC - 1)
            back(0, TC - 2)
            back(0, TC - 1)

            pe.wait_ge(y_out, TC)
            pe.wait_ge(ecum_done, TC)
            with pe.Fori(0, AH) as h:
                pe.wait_ge(vc_done, h + 1)
                pe.wait_ge(at_lo, h * TC)
                for k in range(KT):
                    last = nc.tensor.transpose(PS[:, 4 + k // 4, k % 4 * P:(k % 4 + 1) * P], v_c[:, k * P:(k + 1) * P], ident)
                last.then_inc(v_tr, 1)

                def scores(s):
                    for t in range(2):
                        if s >= 1:
                            pe.wait_ge(exp_done, h * 16 + (2 * s + t - 1))
                        r = slice(t * HD, (t + 1) * HD)
                        qs = slice(s * P, (s + 1) * P)
                        for half in range(2):
                            o, kk = PS[:, 2 * t + half], slice(half * HALF, (half + 1) * HALF)
                            nc.tensor.matmul(o, q_h[r, qs], k_h[r, kk], start=True, stop=False)
                            nc.tensor.matmul(o, q_h[r, qs], k_l[r, kk], start=False, stop=False)
                            last = nc.tensor.matmul(o, q_l[r, qs], k_h[r, kk], start=False, stop=True)
                        last.then_inc(sc_done, 1)

                def turn(s):
                    pe.wait_ge(comb_done, h * TC + (s + 1))
                    if s == 0:
                        pe.wait_ge(v_lo, h + 1)
                    else:
                        pe.wait_ge(at_lo, h * TC + s)
                    for k in range(KT):
                        last = nc.tensor.transpose(PS[:, 4 + k // 4, k % 4 * P:(k % 4 + 1) * P], att[:, s % 2, k * P:(k + 1) * P], ident)
                    last.then_inc(at_tr, 1)

                def values(qh):
                    pe.wait_ge(at_lo, h * TC + (4 * qh + 4))
                    pe.wait_ge(o_done, h * 2)
                    for k in range(KT):
                        o = PS[:, 6 + qh]
                        nc.tensor.matmul(o, v_h[:, k], aT_h[:, k], start=k == 0, stop=False)
                        nc.tensor.matmul(o, v_h[:, k], aT_l[:, k], start=False, stop=False)
                        last = nc.tensor.matmul(o, v_l[:, k], aT_h[:, k], start=False, stop=k == KT - 1)
                    last.then_inc(pv_done, 1)

                pe.wait_ge(qk_lo, h * 2 + 2)
                for s in range(TC):
                    scores(s)
                    if s == 5:
                        values(0)
                    if s >= 1:
                        turn(s - 1)
                turn(TC - 1)
                values(1)

            pe.wait_ge(o_done, 2 * AH)
            for g in range(6):
                if g < 2:
                    pe.wait_ge(gsum_done, g + 1)
                else:
                    pe.wait_ge(gsq_done, 3 + g)
                src, inv = (gsq[:, 2 * g], INV256) if g < 2 else (gsq[:, 2 + g], INV128)
                for t in range(TC):
                    last = nc.tensor.matmul(PS[:, 6, 8 * g + t:8 * g + t + 1], src[:, t * P:(t + 1) * P], cst[:, inv:inv + 1], start=True, stop=True)
            last.then_inc(grow_done, 1)
            pe.wait_ge(groot_done, 1)
            for g in range(6):
                if g >= 2:
                    pe.wait_ge(gs_free, (2, 4, 5, 6)[g - 2])
                for t in range(TC):
                    last = nc.tensor.matmul(PS[:, 2 * (g % 2) + t // 4, t % 4 * P:(t % 4 + 1) * P],
                                            rg[:, 2, 8 * g + t:8 * g + t + 1].to_broadcast([P, P]), ident, start=True, stop=True)
                last.then_inc(gs_done, 1)
            pe.wait_ge(gs_free, KT)

            proj(0, B_OUT, e=2)
            pe.wait_ge(msum_done, 1)
            for t in range(2):
                last = nc.tensor.matmul(PS[:, 6, t:t + 1], qx[:, 4, t * P:(t + 1) * P], cst[:, INV1024:INV1024 + 1], start=True, stop=True)
            last.then_inc(mrow_done, 1)
            proj(0, B_OUT + 1)
            out2 = (x_done, XB[2] - KT - B_OUT)
            with pe.Fori(1, 4) as i:
                proj(i, B_OUT, free=out2)
                proj(i, B_OUT + 1, free=out2)
            pe.wait_ge(mroot_done, 1)
            for t in range(2):
                last = nc.tensor.matmul(PS[:, 7, t * P:(t + 1) * P], rm[:, 2, t:t + 1].to_broadcast([P, P]), ident, start=True, stop=True)
            last.then_inc(mspread_done, 1)
            pe.wait_ge(mem_lo, 1)
            proj(0, B_KV, mem_h, mem_l, M, free=out2)
            root_rows(2)
            proj(0, B_KV + 1, mem_h, mem_l, M, free=out2)
            root_spread(2)
            out3 = (blk_free, -KT)
            with pe.Fori(1, 8) as i:
                proj(i, B_KV, mem_h, mem_l, M, free=out3)
                proj(i, B_KV + 1, mem_h, mem_l, M, free=out3)
            pe.wait_ge(x_lo, 4 * KT)
            with pe.Fori(0, 4) as i:
                proj(i, B_Q, free=out3)
                proj(i, B_Q + 1, free=out3)

            pe.wait_ge(blk_free, B_O - KT)
            with pe.Fori(0, AH) as h:
                pe.wait_ge(cv_copied, h + 1)
                for m in range(2):
                    for e in range(2):
                        last = nc.tensor.transpose(PS[:, 4, m * M + e * P:m * M + (e + 1) * P], cv_c[:, e, m * P:(m + 1) * P], ident)
                last.then_inc(cv_tr, 1)

                def scores(s):
                    pe.wait_ge(cexp_done, h * TC + max(s - 1, 0))
                    o, qs = PS[:, s % 2, 0:M], slice(s * P, (s + 1) * P)
                    for k in range(2):
                        nc.tensor.matmul(o, cq_h[:, k, qs], ck_h[:, k], start=k == 0, stop=False)
                        nc.tensor.matmul(o, cq_h[:, k, qs], ck_l[:, k], start=False, stop=False)
                        last = nc.tensor.matmul(o, cq_l[:, k, qs], ck_h[:, k], start=False, stop=k == 1)
                    last.then_inc(cs_done, 1)

                def turn(s):
                    pe.wait_ge(cnorm_done, h * TC + (s + 1))
                    pe.wait_ge(cp_lo, h * TC + max(s - 1, 0))
                    for m in range(2):
                        last = nc.tensor.transpose(PS[:, 2 + s % 2, m * P:(m + 1) * P], cp[:, s % 4, m * P:(m + 1) * P], ident)
                    last.then_inc(cp_tr, 1)

                pe.wait_ge(c_lo, h * 2 + 2)
                for s in range(TC):
                    scores(s)
                    if s >= 1:
                        turn(s - 1)
                turn(TC - 1)
                pe.wait_ge(cv_lo, h + 1)
                for half in range(2):
                    pe.wait_ge(cp_lo, h * TC + (4 * half + 4))
                    for e in range(2):
                        pe.wait_ge(co_done, h * 4 + (e + 1) * half)
                        o, tok = PS[:, 6 + e], slice(half * HALF, (half + 1) * HALF)
                        for m in range(2):
                            ev = slice(e * P, (e + 1) * P)
                            nc.tensor.matmul(o, cv_h[:, m, ev], cpT_h[:, m, tok], start=m == 0, stop=False)
                            nc.tensor.matmul(o, cv_h[:, m, ev], cpT_l[:, m, tok], start=False, stop=False)
                            last = nc.tensor.matmul(o, cv_l[:, m, ev], cpT_h[:, m, tok], start=False, stop=m == 1)
                        last.then_inc(cpv_done, 1)

            pe.wait_ge(co_done, 4 * AH)
            proj(0, B_O, e=4)
            proj(0, B_O + 1)
            out4 = (x_done, XB[3] - KT - B_O)
            with pe.Fori(1, 4) as i:
                proj(i, B_O, free=out4)
                proj(i, B_O + 1, free=out4)
            pe.wait_ge(x_done, XB[3])
            ffn(1, 3, 5)
            root_rows(4)
            root_spread(4)

        @block.vector
        def _(dve):
            own = Steps(dve, dve_own)

            def low_x(e, k, src=None):
                dve.wait_ge(x_hi, KT * e + k + 1)
                nc.vector.tensor_tensor(XL[:, k], X[:, k] if src is None else src, XH[:, k].bitcast(F32), ALU.subtract).then_inc(x_lo, 1)

            def root(n):
                dve.wait_ge(rs_done, n + 1)
                own.done(nc.vector.tensor_scalar(rn[:, 0, 0:TC], PS[:, 6, 0:TC], EPS, None, ALU.add))
                nc.vector.reciprocal(rn[:, 1, 0:TC], rn[:, 0, 0:TC]).then_inc(rs_inv, 1)
                dve.wait_ge(rb_done, n + 1)
                nc.vector.tensor_copy(RB[:], PS[:, 4:6].rearrange("p a b -> p (a b)")).then_inc(r_ready, 1)
                dve.wait_ge(r_ready, n + 1)

            def ffn(f, n, gain, before, after):
                c0, u0 = f * FC, 2 * f * FC

                def split_gu(i, c, pieces=range(4)):
                    for q in pieces:
                        dve.wait_ge(gu_hi, i * 8 + (4 * (c0 + c) + q + 1))
                        for k in range(2 * q, 2 * q + 2):
                            last = nc.vector.scalar_tensor_tensor(
                                out=wgu_l[:, k], in0=wgu_raw[:, c % 2, k], scalar=par[:, gain + k:gain + k + 1],
                                in1=wgu_h[:, k].bitcast(F32), op0=ALU.mult, op1=ALU.subtract)
                        last.then_inc(gu_lo, 1)

                def split_wd(i, c):
                    dve.wait_ge(wd_hi, i * 2 + (c0 + c + 1))
                    nc.vector.tensor_tensor(wd_l[:, c], wd_raw[:, c], wd_h[:, c].bitcast(F32),
                                            ALU.subtract).then_inc(wd_lo, 1)

                def unit(i, u):
                    b, tok = 2 * (u % 2), slice(u % 2 * HALF, (u % 2 + 1) * HALF)
                    dve.wait_ge(unit_done, i * 4 + (u0 + u + 1))
                    nc.vector.tensor_tensor(tg[:, u % 2], PS[:, b], RB[:, tok], ALU.mult).then_inc(tg_done, 1)
                    nc.vector.tensor_tensor(tu[:, u % 2], PS[:, b + 1], RB[:, tok], ALU.mult).then_inc(unit_free, 1)
                    dve.wait_ge(silu_done, i * 4 + (u0 + u + 1))
                    dve.wait_ge(unit_free, i * 4 + (u0 + u + 1))
                    nc.vector.tensor_tensor(ta[:, u % 2], tsl[:, u % 2], tu[:, u % 2], ALU.mult).then_inc(ta_done, 1)
                    dve.wait_ge(hid_hi, i * 4 + (u0 + u + 1))
                    nc.vector.tensor_tensor(hid_l[:, u // 2, tok], ta[:, u % 2], hid_h[:, u // 2, tok].bitcast(F32),
                                            ALU.subtract).then_inc(hid_lo, 1)

                def add_down(i, m):
                    dve.wait_ge(down_done, i * KT + (KT * PAIRS * f + m + 1))
                    b = 4 + 2 * (m % 2)
                    nc.vector.scalar_tensor_tensor(out=X[:, m], in0=PS[:, b:b + 2].rearrange("p a b -> p (a b)"), scalar=0.5, in1=X[:, m],
                                                   op0=ALU.mult, op1=ALU.add).then_inc(x_done, 1)

                split_gu(0, 0)
                before()
                root(n)

                def pair(i, last=False):
                    unit(i, 0)
                    split_wd(i, 0)
                    split_wd(i, 1)
                    split_gu(i, 1)
                    unit(i, 1)
                    unit(i, 2)
                    if not last:
                        split_gu(i, 2, range(3))
                    unit(i, 3)
                    if not last:
                        split_gu(i, 2, range(3, 4))
                        for m in range(KT):
                            add_down(i, m)

                pair(0)
                with dve.Fori(1, PAIRS - 1) as i:
                    pair(i)
                pair(PAIRS - 1, last=True)
                after(add_down)

            def split_weights(i, b, gain, src):
                dve.wait_ge(wp_hi, i * 2 + (b + 1))
                for k in range(KT):
                    last = nc.vector.scalar_tensor_tensor(
                        out=wp_l[:, b % 2, k], in0=wp_raw[:, b % 2, k], scalar=src[:, gain + k:gain + k + 1],
                        in1=wp_h[:, b % 2, k].bitcast(F32), op0=ALU.mult, op1=ALU.subtract)
                last.then_inc(wp_lo, 1)

            def banks(b):
                return PS[:, 2 * (b % 2):2 * (b % 2) + 2].rearrange("p a b -> p (a b)")

            def to_mixer(add_down):
                split_weights(0, 0, G_MIX, par)
                for m in range(KT):
                    add_down(PAIRS - 1, m)
                    if m:
                        low_x(1, m - 1)
                low_x(1, KT - 1)
                dve.wait_ge(s_wdt, 16)
                nc.vector.tensor_tensor(w_dtg[:], dt_raw[:], par[:, G_MIX:G_MIX + KT].unsqueeze(2).to_broadcast([P, KT, 16]),
                                        ALU.mult).then_inc(wdt_done, 1)
                root(1)

            def x_loaded():
                for k in range(KT):
                    low_x(0, k)

            dve.wait_ge(s_par, 16)
            ffn(0, 0, G_FFN1, x_loaded, to_mixer)

            dve.memset(craw[:, 0:2], 0.0)
            own.done(dve.memset(craw[:, S + 2:S + 4], 0.0))
            n_conv = 5

            def conv_block(i, j):
                dve.wait_ge(blk_done, i * 2 + j + 1)
                own_blk = i * 2 + j + 1
                nc.vector.tensor_tensor(craw[:, 2:S + 2], banks(j), RB[:], ALU.mult).then_inc(blk_free, 1)
                dve.wait_ge(blk_free, own_blk)
                if j == 1:
                    dve.wait_ge(conv_silu, i * 2)
                else:
                    dve.wait_ge(conv_silu, i * 2)
                a = conv_acc[:, j]
                own.done(nc.vector.tensor_scalar(a, craw[:, 0:S], par[:, one(i * 10 + (CONVW + 5 * j))], None, ALU.mult))
                for t in range(1, 5):
                    ins = nc.vector.scalar_tensor_tensor(out=a, in0=craw[:, t:t + S], scalar=par[:, one(i * 10 + (CONVW + 5 * j + t))],
                                                         in1=a, op0=ALU.mult, op1=ALU.add)
                    if t < 4:
                        own.done(ins)
                    else:
                        ins.then_inc(conv_done, 1)

            base = own.n
            with dve.Fori(0, (B_Z - B_XBC) // 2) as i:
                for j in range(2):
                    own.n = i * 8 + (base + 4 * j)
                    split_weights(i, j + 1, G_MIX, par)
                    conv_block(i, j)
            own.n = base + 4 * 8
            dve.wait_ge(dt_done, 1)
            own.done(nc.vector.tensor_tensor(dt_raw[:], PS[:, 7, 0:P].rearrange("p (c h) -> p c h", c=TC),
                                             rn[:, 2, 0:TC].unsqueeze(2).to_broadcast([P, TC, 16]), ALU.mult))
            dve.tensor_tensor(dt_raw[:], dt_raw[:], par[:, DTBIAS:DTBIAS + 16].unsqueeze(1).to_broadcast([P, TC, 16]),
                              ALU.add).then_inc(dt_out, 1)
            with dve.Fori(0, (B_V - B_Z) // 2) as i:
                for j in range(2):
                    split_weights(i, B_Z + j + 1, G_MIX, par)
                    dve.wait_ge(blk_done, i * 2 + (B_Z + j + 1))
                    dve.wait_ge(conv_silu, i * 2 + (B_Z + j - 1))
                    nc.vector.tensor_tensor(conv_acc[:, j], banks(j), RB[:], ALU.mult).then_inc(blk_free, 1)
            with dve.Fori(0, (B_QK - B_V) // 2) as i:
                for j in range(2):
                    split_weights(i, B_V + j + 1, G_MIX, par)
                    dve.wait_ge(blk_done, i * 2 + (B_V + j + 1))
                    nc.vector.tensor_tensor(vo[:, one(i * 2 + j)].rearrange("p o s -> p (o s)"), banks(j), RB[:], ALU.mult).then_inc(blk_free, 1)

            def turn_qk(i, j, nstep):
                xq = X[:, one(i * 2 + j)].rearrange("p o s -> p (o s)")
                t = craw[:, 0:S]
                dve.wait_ge(swap_done, i * 2 + (j + 1))
                own.n = nstep
                dve.wait_ge(qk_ready, i * 2 + j)
                own.mark(nc.vector.tensor_tensor(t, PS[:, 4 + 2 * (j % 2):6 + 2 * (j % 2)].rearrange("p a b -> p (a b)"), rope[:, 1], ALU.mult))
                own.done(nc.vector.tensor_tensor(xq, xq, rope[:, 0], ALU.mult))
                nc.vector.tensor_tensor(xq, xq, t, ALU.add).then_inc(qk_ready, 1)

            def out_qk(i, j):
                dve.wait_ge(blk_done, i * 2 + (B_QK + j + 1))
                nc.vector.tensor_tensor(X[:, one(i * 2 + j)].rearrange("p o s -> p (o s)"), banks(j), RB[:], ALU.mult).then_inc(blk_free, 1)

            dve.wait_ge(s_spill, 16)
            dve.wait_ge(s_rope, 16)
            split_weights(0, B_QK + 1, G_MIX, par)
            out_qk(0, 0)
            base = own.n
            with dve.Fori(0, 3) as i:
                for j in range(2):
                    split_weights(i, B_QK + j + 2, G_MIX, par)
                    out_qk(i, j + 1)
                    turn_qk(i, j, i * 4 + (base + 2 * j))
            out_qk(0, 7)
            turn_qk(0, 6, base + 12)
            turn_qk(0, 7, base + 14)

            t1, t2, ex = etot, cum, w_state
            dve.wait_ge(blk_done, B_OUT)
            nc.vector.tensor_scalar(t1[:], dt_raw[:], -1.0, None, ALU.mult).then_inc(dve_own, 1)
            own.n = own.n + 1
            own.wait()
            nc.vector.tensor_tensor(t1[:], t1[:], dt_raw[:], ALU.max).then_inc(sp_step, 1)
            dve.wait_ge(sp_act, 1)
            dve.tensor_scalar(t1[:], ex[:], 1.0, None, ALU.add).then_inc(sp_step, 1)
            dve.wait_ge(sp_step, 2)
            own.done(nc.vector.tensor_scalar(dt_tmp[:], t1[:], 1.0, None, ALU.subtract))
            own.done(nc.vector.tensor_scalar(dt[:], dt_tmp[:], 0.0, None, ALU.is_equal))
            own.done(nc.vector.tensor_tensor(dt_tmp[:], dt_tmp[:], dt[:], ALU.add))
            dve.wait_ge(sp_act, 2)
            own.done(nc.vector.tensor_tensor(t2[:], t2[:], dt[:], ALU.add))
            own.done(nc.vector.reciprocal(dt_tmp[:], dt_tmp[:]))
            own.done(nc.vector.tensor_tensor(t2[:], t2[:], dt_tmp[:], ALU.mult))
            own.done(nc.vector.tensor_tensor(t2[:], t2[:], ex[:], ALU.mult))
            own.done(nc.vector.tensor_scalar(dt_raw[:], dt_raw[:], 0.0, None, ALU.max))
            own.done(nc.vector.tensor_tensor(dt[:], dt_raw[:], t2[:], ALU.add))
            dve.wait_ge(sp_act, 3)
            own.done(nc.vector.tensor_scalar(rn[:, 1, :], rn[:, 0, :], -1.0, None, ALU.mult))
            dve.tensor_tensor(da[:], dt[:], rn[:, 1, :].unsqueeze(1).to_broadcast([P, TC, 16]), ALU.mult).then_inc(dt_out, 1)
            dve.wait_ge(cum_done, 1)
            own.done(dve.tensor_copy(cum[:], PS[:, 7, 0:P].rearrange("p (c h) -> p c h", c=TC)))
            dve.tensor_tensor(dt_tmp[:], PS[:, 6, 0:P].rearrange("p (c h) -> p c h", c=TC), cum[:], ALU.subtract).then_inc(sp_step, 1)
            dve.wait_ge(sp_act, 4)
            dve.tensor_tensor(w_state[:], w_state[:], dt[:], ALU.mult).then_inc(sp_step, 1)
            nc.vector.memset(carry[:, 0], 0.0)
            dve.memset(prev_b[:, TC - 1], 0.0).then_inc(pb_done, 1)
            dve.wait_ge(sp_act, 5)

            def per_head(t, c, d, n):
                return t[:, one(c), 8 * d:8 * d + 8].rearrange("p o h -> p (o h)").unsqueeze(2).to_broadcast([P, NH, n])

            def heads(ap):
                return ap.rearrange("p (h d) -> p h d", h=NH)

            base = own.n
            with dve.Fori(0, TC - 1) as r:
                c = r * -1 + (TC - 1)
                own.n = r + base
                dve.wait_ge(pb_done, r + 1)
                dst = prev_b[:, one(c - 1)].rearrange("p o (h d) -> p (o h) d", h=NH)
                own.done(dve.tensor_tensor(dst, prev_b[:, one(c)].rearrange("p o (h d) -> p (o h) d", h=NH), per_head(etot, c, 1, HD), ALU.mult))
                dve.wait_ge(st_done, r + 1)
                dve.tensor_tensor(dst, dst, heads(PS[:, 6]), ALU.add).then_inc(pb_done, 1)
            own.n = base + TC - 1

            def first_part(i, c, nstep):
                own.n = nstep
                dve.wait_ge(rows_done, i * 2 + (c + 1))
                cc = i * 2 + c
                if c >= 1 or not isinstance(i, int):
                    dve.wait_ge(y_done, i * 2 + c)
                for d, a in enumerate((arg1, arg2)):
                    own.mark(dve.tensor_tensor(a[:], PS[:, 2 * d:2 * d + 2].rearrange("p a (h l) -> p (a h) l", l=P), per_head(cum, cc, d, P), ALU.subtract))
                own.wait()
                own.done(dve.tensor_scalar(arg2[:], arg2[:], 0.0, None, ALU.min))
                dve.scalar_tensor_tensor(out=arg1[:].rearrange("p h l -> p (h l)"), in0=arg1[:].rearrange("p h l -> p (h l)"), scalar=0.0,
                                         in1=arg2[:].rearrange("p h l -> p (h l)"), op0=ALU.min, op1=ALU.add).then_inc(arg_done, 1)
                dve.wait_ge(cb_done, i * 2 + (c + 1))
                src = PS[:, 5, 256:512].rearrange("p (g l) -> p g l", g=2)
                dve.tensor_tensor(cb[:, 0], src, trif.unsqueeze(1).to_broadcast([P, 2, P]), ALU.mult)
                dve.tensor_tensor(cb[:, 1], src, trib.unsqueeze(1).to_broadcast([P, 2, P]), ALU.mult).then_inc(cb_used, 1)
                dve.wait_ge(cb_used, i * 2 + (c + 1))

            def second_part(i, c):
                dve.wait_ge(e_done, i * 2 + (c + 1))
                e4 = arg1[:].rearrange("p (g r) l -> p g r l", g=2)
                m4 = arg2[:].rearrange("p (g r) l -> p g r l", g=2)
                own.done(dve.tensor_tensor(m4, e4, cb[:, 1].unsqueeze(2).to_broadcast([P, 2, 4, P]), ALU.mult))
                dve.tensor_tensor(e4, e4, cb[:, 0].unsqueeze(2).to_broadcast([P, 2, 4, P]), ALU.mult).then_inc(m_done, 1)

            def third_part(i, c):
                p, cc = c % 2, i * 2 + c
                dve.wait_ge(y_done, i * 2 + (c + 1))
                for k in range(4):
                    ins = dve.scalar_tensor_tensor(out=tmps[:, k], in0=stage[:, p, k], scalar=par[:, DSKIP + k:DSKIP + k + 1],
                                                   in1=PS[:, 7, k * P:(k + 1) * P], op0=ALU.mult, op1=ALU.add)
                own.done(ins)
                dve.tensor_tensor(zy[:, :, chunk(cc)], zy[:, :, chunk(cc)], tmps[:], ALU.mult).then_inc(y_out, 1)
                dve.wait_ge(st2_done, i * 2 + (c + 1))
                own.done(dve.tensor_tensor(heads(carry[:, 1 - p]), heads(carry[:, p]), per_head(etot, cc, 0, HD), ALU.mult))
                dve.tensor_tensor(carry[:, 1 - p], carry[:, 1 - p], PS[:, 6], ALU.add).then_inc(carry_done, 1)
                dve.wait_ge(carry_done, i * 2 + (c + 1))

            base = own.n
            with dve.Fori(0, TC // 2) as i:
                for c in range(2):
                    first_part(i, c, i * 12 + (base + 6 * c))
                    second_part(i, c)
                    third_part(i, c)
            own.n = base + 6 * TC

            dve.wait_ge(y_out, TC)
            lv = par[:, LAM:LAM + 4 * HD].rearrange("p (a b d) -> p a b d", a=2, b=2)
            own.done(dve.tensor_tensor(lam_t[:], lv[:, :, 0], lv[:, :, 1], ALU.mult))
            dve.tensor_reduce(lam[:, 0:2], lam_t[:], AX.X, ALU.add).then_inc(lam_sum, 1)
            dve.wait_ge(lam_exp, 1)
            own.done(dve.tensor_tensor(lam[:, 4:5], lam[:, 2:3], lam[:, 3:4], ALU.subtract))
            own.done(dve.tensor_scalar(lam[:, 5:6], lam[:, 4:5], LAMBDA_INIT, None, ALU.add))
            dve.tensor_copy(g_out[:, 0:4], par[:, G_SSD:G_SSD + 4])
            dve.memset(g_out[:, 8:16], 1.0)
            dve.tensor_scalar(g_out[:, 4:8], par[:, G_SUB:G_SUB + 1].to_broadcast([P, 4]), 1.0 - LAMBDA_INIT, None, ALU.mult).then_inc(g_done, 1)

            base = own.n
            PER_HEAD = 5 * TC
            with dve.Fori(0, AH) as h:
                own.n = h * PER_HEAD + base
                for t, (hi, lo) in enumerate(((q_h, q_l), (k_h, k_l))):
                    dve.wait_ge(qk_hi, h * 2 + (t + 1))
                    dve.tensor_tensor(lo[:], X[:, one(h + AH * t)].rearrange("p o s -> p (o s)"), hi[:].bitcast(F32), ALU.subtract).then_inc(qk_lo, 1)
                dve.wait_ge(v_hi, h + 1)
                dve.tensor_tensor(v_l[:], PS[:, 4:6].rearrange("p a (k e) -> p (a k) e", e=P), v_h[:].bitcast(F32), ALU.subtract).then_inc(v_lo, 1)

                def largest(s):
                    for t in range(2):
                        dve.wait_ge(sc_done, h * 16 + (2 * s + t + 1))
                        own.done(dve.tensor_reduce(stat[:, s % 2, t, 0:1], PS[:, 2 * t:2 * t + 2].rearrange("p a b -> p (a b)"), AX.X, ALU.max))
                        dve.tensor_scalar(stat[:, s % 2, 2 + t, 0:1], stat[:, s % 2, t, 0:1], -0.125, None, ALU.mult).then_inc(nm_done, 1)

                def combine(s):
                    z = stat[:, s % 2]
                    dve.wait_ge(exp_done, h * 16 + (2 * s + 2))
                    own.done(dve.reciprocal(z[:, 6:8, 0:1], z[:, 4:6, 0:1]))
                    own.done(dve.tensor_scalar(z[:, 7, 1:2], z[:, 7, 0:1], lam[:, 5:6], None, ALU.mult))
                    own.done(dve.tensor_scalar(pr[:, s % 2, 1], pr[:, s % 2, 1], z[:, 7, 1:2], None, ALU.mult))
                    dve.wait_ge(at_tr, h * TC + max(s - 1, 0))
                    dve.scalar_tensor_tensor(out=att[:, s % 2], in0=pr[:, s % 2, 0], scalar=z[:, 6, 0:1], in1=pr[:, s % 2, 1],
                                             op0=ALU.mult, op1=ALU.subtract).then_inc(comb_done, 1)

                def low(s):
                    dve.wait_ge(at_hi, h * TC + (s + 1))
                    sl = slice(s % 4 * P, (s % 4 + 1) * P)
                    dve.tensor_tensor(aT_l[:, :, sl], PS[:, 4:6].rearrange("p a (k q) -> p (a k) q", q=P), aT_h[:, :, sl].bitcast(F32),
                                      ALU.subtract).then_inc(at_lo, 1)

                def values(qh):
                    dve.wait_ge(pv_done, h * 2 + (qh + 1))
                    dve.tensor_scalar(vo[:, one(h), qh * HALF:(qh + 1) * HALF].rearrange("p o s -> p (o s)"), PS[:, 6 + qh],
                                      1.0, None, ALU.mult).then_inc(o_done, 1)

                for s in range(TC + 2):
                    if s < TC:
                        largest(s)
                    if 1 <= s <= TC:
                        combine(s - 1)
                    if s >= 2:
                        low(s - 2)
                    if s == 6:
                        values(0)
                values(1)
            own.n = base + PER_HEAD * AH

            dve.wait_ge(grow_done, 1)
            own.done(dve.tensor_scalar(rg[:, 0], PS[:, 6, 0:48], EPS, None, ALU.add))
            dve.reciprocal(rg[:, 1], rg[:, 0]).then_inc(ginv_done, 1)
            split_weights(0, B_OUT, 0, g_out)
            for g in range(6):
                dve.wait_ge(gs_done, g + 1)
                r = PS[:, 2 * (g % 2):2 * (g % 2) + 2].rearrange("p a b -> p (a b)")
                tiles_ = [zy[:, 2 * g], zy[:, 2 * g + 1]] if g < 2 else [vo[:, g - 2]]
                k0 = 2 * g if g < 2 else 2 + g
                for n_, y in enumerate(tiles_):
                    dve.tensor_tensor(y, y, r, ALU.mult).then_inc(gs_free, 1)
                for n_, y in enumerate(tiles_):
                    low_x(2, k0 + n_, y)
            dve.wait_ge(mem_hi, 1)
            dve.tensor_tensor(mem_l[:], memX[:], mem_h[:].bitcast(F32), ALU.subtract).then_inc(mem_lo, 1)
            dve.wait_ge(mrow_done, 1)
            own.done(dve.tensor_scalar(rm[:, 0], PS[:, 6, 0:2], EPS, None, ALU.add))
            dve.reciprocal(rm[:, 1], rm[:, 0]).then_inc(minv_done, 1)

            def residual(n, b0, b1, gain, src):
                def add(i, j):
                    dve.wait_ge(blk_done, i * 2 + (b0 + j + 1))
                    x = X[:, one(i * 2 + j)].rearrange("p o s -> p (o s)")
                    dve.tensor_tensor(x, banks(j), x, ALU.add).then_inc(x_done, 1)
                with dve.Fori(0, (b1 - b0) // 2 - 1) as i:
                    for j in range(2):
                        split_weights(i, b0 + j + 1, gain, src)
                        add(i, j)
                split_weights(0, b1 - 1, gain, src)
                add(KT // 2 - 1, 0)
                add(KT // 2 - 1, 1)

            for q in range(4):
                dve.wait_ge(s_back[q], 16)
            residual(2, B_OUT, B_KV, 0, g_out)
            split_weights(0, B_KV, G_MEM, par)
            dve.wait_ge(mspread_done, 1)
            dve.tensor_copy(RM[:], PS[:, 7, 0:M]).then_inc(mr_done, 1)
            dve.wait_ge(mr_done, 1)
            dve.wait_ge(rs_done, 3)
            own.done(nc.vector.tensor_scalar(rn[:, 0, 0:TC], PS[:, 6, 0:TC], EPS, None, ALU.add))
            nc.vector.reciprocal(rn[:, 1, 0:TC], rn[:, 0, 0:TC]).then_inc(rs_inv, 1)

            def kv_out(i, j):
                dve.wait_ge(blk_done, i * 2 + (B_KV + j + 1))
                dve.tensor_tensor(kv[:, one(i * 2 + j)].rearrange("p o m -> p (o m)"), PS[:, 2 * j, 0:M], RM[:], ALU.mult).then_inc(blk_free, 1)

            split_weights(0, B_KV + 1, G_MEM, par)
            kv_out(0, 0)
            for k in range(KT):
                low_x(3, k)
            with dve.Fori(0, (B_Q - B_KV) // 2 - 1) as i:
                split_weights(i, B_KV + 2, G_MEM, par)
                kv_out(i, 1)
                split_weights(i, B_KV + 3, G_MEM, par)
                dve.wait_ge(blk_done, i * 2 + (B_KV + 3))
                dve.tensor_tensor(kv[:, one(i * 2 + 2)].rearrange("p o m -> p (o m)"), PS[:, 0, 0:M], RM[:], ALU.mult).then_inc(blk_free, 1)
            split_weights(0, B_Q, G_XQ, par)
            kv_out(7, 1)
            dve.wait_ge(rb_done, 3)
            dve.tensor_copy(RB[:], PS[:, 4:6].rearrange("p a b -> p (a b)")).then_inc(r_ready, 1)
            dve.wait_ge(r_ready, 3)

            def q_out(i, j):
                dve.wait_ge(blk_done, i * 2 + (B_Q + j + 1))
                dve.tensor_tensor(qx[:, one(i * 2 + j)].rearrange("p o s -> p (o s)"), banks(j), RB[:], ALU.mult).then_inc(blk_free, 1)
            with dve.Fori(0, (B_O - B_Q) // 2 - 1) as i:
                for j in range(2):
                    split_weights(i, B_Q + j + 1, G_XQ, par)
                    q_out(i, j)
            split_weights(0, B_O - 1, G_XQ, par)
            q_out(3, 0)
            q_out(3, 1)

            base = own.n
            PER = 2 * TC + TC
            with dve.Fori(0, AH) as h:
                own.n = h * (2 * TC) + base
                dve.wait_ge(c_hi, h * 2 + 1)
                dve.tensor_tensor(cq_l[:], qx[:, bass.ds(h * 2, 2)], cq_h[:].bitcast(F32), ALU.subtract).then_inc(c_lo, 1)
                dve.wait_ge(c_hi, h * 2 + 2)
                dve.tensor_tensor(ck_l[:], kv[:, bass.ds(h * 2, 2)], ck_h[:].bitcast(F32), ALU.subtract).then_inc(c_lo, 1)
                dve.wait_ge(cv_hi, h + 1)
                dve.tensor_tensor(cv_l[:], PS[:, 4].rearrange("p (m e) -> p m e", m=2), cv_h[:].bitcast(F32), ALU.subtract).then_inc(cv_lo, 1)

                def largest(s):
                    dve.wait_ge(cs_done, h * TC + (s + 1))
                    own.done(dve.tensor_reduce(cst_[:, 0, s:s + 1], PS[:, s % 2, 0:M], AX.X, ALU.max))
                    dve.tensor_scalar(cst_[:, 0, s:s + 1], cst_[:, 0, s:s + 1], -0.0625, None, ALU.mult).then_inc(cnm_done, 1)

                def normalise(s):
                    dve.wait_ge(cexp_done, h * TC + (s + 1))
                    own.done(dve.reciprocal(cst_[:, 1, s:s + 1], cst_[:, 1, s:s + 1]))
                    dve.tensor_scalar(cp[:, s % 4], cp[:, s % 4], cst_[:, 1, s:s + 1], None, ALU.mult).then_inc(cnorm_done, 1)

                def low(s):
                    dve.wait_ge(cp_hi, h * TC + (s + 1))
                    sl = slice(s * P, (s + 1) * P)
                    dve.tensor_tensor(cpT_l[:, :, sl], PS[:, 2 + s % 2, 0:M].rearrange("p (m q) -> p m q", m=2), cpT_h[:, :, sl].bitcast(F32),
                                      ALU.subtract).then_inc(cp_lo, 1)

                for s in range(TC + 2):
                    if s < TC:
                        largest(s)
                    if 1 <= s <= TC:
                        normalise(s - 1)
                    if s >= 2:
                        low(s - 2)
                for half in range(2):
                    for e in range(2):
                        dve.wait_ge(cpv_done, h * 4 + (2 * half + e + 1))
                        dve.tensor_scalar(qx[:, one(h * 2 + e), half * HALF:(half + 1) * HALF].rearrange("p o s -> p (o s)"), PS[:, 6 + e],
                                          1.0, None, ALU.mult).then_inc(co_done, 1)
            own.n = base + 2 * TC * AH
            split_weights(0, B_O, 8, g_out)
            for k in range(KT):
                low_x(4, k, qx[:, k])
            residual(3, B_O, B_END, 8, g_out)

            def to_ffn2():
                for k in range(KT):
                    low_x(5, k)

            def to_end(add_down):
                for m in range(KT):
                    add_down(PAIRS - 1, m)
                root(4)
                for k in range(KT):
                    dve.scalar_tensor_tensor(out=X[:, k], in0=X[:, k], scalar=par[:, G_FIN + k:G_FIN + k + 1], in1=RB[:],
                                             op0=ALU.mult, op1=ALU.mult).then_inc(fin_done, 1)

            ffn(1, 3, G_FFN2, to_ffn2, to_end)


def lay_out(inputs):
    a = {k: np.asarray(v) for k, v in inputs.items()}

    def tiles(v):
        return v.reshape(-1, P).T

    def blocks(w):
        return np.ascontiguousarray(w.reshape(KT, P, -1, P).transpose(2, 1, 0, 3))

    def gate_up(g, u):
        return np.ascontiguousarray(np.stack([g.reshape(KT, P, FC, P), u.reshape(KT, P, FC, P)], 3).transpose(2, 1, 0, 3, 4))

    def rows(v):
        return np.broadcast_to(v.reshape(1, -1), (P, v.size))

    par = np.concatenate([
        tiles(a["ffn1_norm_g"][0]), tiles(a["mix_norm_g"][0]), tiles(a["xattn_norm_g"][0]), tiles(a["mem_norm_g"][0]),
        tiles(a["ffn2_norm_g"][0]), tiles(a["final_norm_g"]), tiles(a["ssd_norm_g"][0]), tiles(a["diff_subln_g"][0]),
        a["conv_w"][0].reshape(5, KT, P).transpose(2, 1, 0).reshape(P, 40), tiles(a["conv_b"][0]),
        tiles(np.repeat(a["D_skip"][0], 64)),
        rows(np.concatenate([a["dt_bias_fwd"][0], a["dt_bias_bwd"][0]])),
        rows(np.concatenate([a["A_log_fwd"][0], a["A_log_bwd"][0]])),
        rows(np.concatenate([a["lambda_q1"][0], a["lambda_k1"][0], a["lambda_q2"][0], a["lambda_k2"][0]])),
    ], 1)
    assert par.shape == (P, NPAR)

    cst = np.zeros((P, NCST), np.float32)
    cst[:, IDENT:IDENT + P] = np.eye(P)
    cst[:, ONES:ONES + P] = 1
    cst[:, TRIF:TRIF + P] = np.triu(np.ones((P, P)))
    cst[:, TRIB:TRIB + P] = np.tril(np.ones((P, P)))
    cst[:, INV1024], cst[:, INV256], cst[:, INV128] = 1 / 1024, 1 / 256, 1 / 128
    inv = (1.0 / np.float32(500000.0) ** (np.arange(0, 16, 2, dtype=np.float32) / np.float32(16))).astype(np.float32)
    ang = (np.arange(S, dtype=np.float32)[:, None] * inv[None]).astype(np.float32)
    rope = np.zeros((P, 2, S), np.float32)
    rope[:, 0] = 1
    for r in range(P):
        d = r % 64
        if d < 16:
            partner = r + 8 if d < 8 else r - 8
            rope[r, 0] = np.cos(ang[:, d % 8])
            rope[r, 1] = np.sin(ang[:, d % 8]) * (-1 if d < 8 else 1)
            cst[partner, ROPEP + r] = 1
    w = a["w_in"][0]
    w_in = blocks(np.concatenate([w[:, 512:1536], w[:, 0:512], w[:, 2576:3088], w[:, 1552:2576]], 1))
    return {
        "xT": np.ascontiguousarray(a["x"][0].T.reshape(KT, P, S).transpose(1, 0, 2)),
        "memT": np.ascontiguousarray(a["mem"][0].T.reshape(KT, P, 256).transpose(1, 0, 2)),
        "par": np.ascontiguousarray(par), "cst": cst, "rope": rope,
        "wgu1": gate_up(a["ffn1_w_gate"][0], a["ffn1_w_up"][0]), "wd1": np.ascontiguousarray(a["ffn1_w_down"][0].reshape(FC, P, D)),
        "wgu2": gate_up(a["ffn2_w_gate"][0], a["ffn2_w_up"][0]), "wd2": np.ascontiguousarray(a["ffn2_w_down"][0].reshape(FC, P, D)),
        "w_in": w_in, "w_dt": np.ascontiguousarray(w[:, 1536:1552].reshape(KT, P, 16).transpose(1, 0, 2)),
        "w_out": blocks(a["w_out"][0]), "w_q": blocks(a["xattn_w_q"][0]), "w_kv": blocks(a["xattn_w_kv"][0]),
        "w_o": blocks(a["xattn_w_o"][0]),
    }


def kernel(**inputs):
    import concourse.bacc as bacc
    from concourse.bass_utils import run_bass_kernel_spmd

    nc = bacc.Bacc("TRN2", target_bir_lowering=False, num_devices=1)
    arrays = {f"in_{k}": v for k, v in lay_out(inputs).items()}
    args = [nc.dram_tensor(k, v.shape, mybir.dt.from_np(v.dtype), kind="ExternalInput").ap() for k, v in arrays.items()]
    args.append(nc.dram_tensor("out_yT", (P, KT, S), F32, kind="ExternalOutput").ap())
    build(nc, *args)
    r = run_bass_kernel_spmd(nc, [arrays], core_ids=[0])
    return r.results[0]["out_yT"].transpose(2, 1, 0).reshape(1, S, D)
```

```python
from contextlib import ExitStack

import concourse.bass as bass
import numpy as np
from concourse import mybir

F32 = mybir.dt.float32
F32R = mybir.dt.float32r
ACT = mybir.ActivationFunctionType
ALU = mybir.AluOpType
AX = mybir.AxisListType

P = 128
D = 1024
KT = D // P
S = 1024
HALF = 512
TC = S // P
FF = 2816
FC = FF // P
PAIRS = FC // 2
NH = 8
HD = 64
AH = 4
M = 256
LAMBDA_INIT = 0.8 - 0.6
B_XBC, B_Z, B_V, B_QK, B_OUT, B_KV, B_Q, B_O, B_END = 0, 8, 12, 16, 24, 32, 48, 56, 64
EPS = 1e-5
XB = [0, KT * PAIRS, KT * PAIRS + KT, KT * PAIRS + 2 * KT, 2 * KT * PAIRS + 2 * KT]

G_FFN1, G_MIX, G_XQ, G_MEM, G_FFN2, G_FIN = (8 * i for i in range(6))
G_SSD, G_SUB = 48, 52
CONVW, CONVB, DSKIP, DTBIAS, ALOG, LAM = 53, 93, 101, 105, 121, 137
NPAR = LAM + 4 * 64
IDENT, ONES, TRIF, TRIB, ROPEP = (128 * i for i in range(5))
INV1024, INV256, INV128 = 640, 641, 642
NCST = 643


class Steps:

    def __init__(self, eng, sem):
        self.eng, self.sem, self.n = eng, sem, 0

    def mark(self, instruction):
        instruction.then_inc(self.sem, 1)
        self.n = self.n + 1

    def wait(self):
        self.eng.wait_ge(self.sem, self.n)

    def done(self, instruction):
        self.mark(instruction)
        self.wait()


def build(nc, xT, memT, par_d, cst_d, rope_d, wgu1, wd1, wgu2, wd2, w_in, w_dt, w_out, w_q, w_kv, w_o, out):
    ctx = ExitStack()
    at = [16512]

    def place(name, shape, dt, offset=None):
        size = int(np.prod(shape[1:])) * 4
        if offset is None:
            offset = at[0]
            at[0] += -(-size // 32) * 32
        return nc.alloc_sbuf_tensor_at(name, shape, dt, offset=offset), offset

    X, X0 = place("X", [P, KT, S], F32)
    XR, _ = place("XR", [P, KT, S], F32R, X0)
    XH, XH0 = place("XH", [P, KT, S], F32R)
    XL, XL0 = place("XL", [P, KT, S], F32R)
    RB, _ = place("RB", [P, S], F32)
    par, _ = place("par", [P, NPAR], F32)
    cst, _ = place("cst", [P, NCST], F32)
    rn, _ = place("rn", [P, 3, 16], F32)
    W0 = at[0]

    wgu_raw, o = place("wgu_raw", [P, 2, KT, 2, P], F32)
    wgu_h, o_gh = place("wgu_h", [P, KT, 2, P], F32R)
    wgu_l, o_gl = place("wgu_l", [P, KT, 2, P], F32R)
    wd_raw, _ = place("wd_raw", [P, 2, D], F32)
    wd_h, _ = place("wd_h", [P, 2, D], F32R)
    wd_l, _ = place("wd_l", [P, 2, D], F32R)
    hid_h, _ = place("hid_h", [P, 2, S], F32R)
    hid_l, _ = place("hid_l", [P, 2, S], F32R)
    T0 = at[0]
    tg, _ = place("tg", [P, 2, HALF], F32)
    tsl, _ = place("tsl", [P, 2, HALF], F32)
    tu, _ = place("tu", [P, 2, HALF], F32)
    ta, _ = place("ta", [P, 2, HALF], F32)
    assert at[0] <= nc.sbuf_usable_end, at[0]
    sq, _ = place("sq", [P, 2, S], F32, T0)
    ssum, _ = place("ssum", [P, S], F32, T0 + 2 * S * 4)

    wp_raw, _ = place("wp_raw", [P, 2, KT, P], F32, W0)
    wp_h, _ = place("wp_h", [P, 2, KT, P], F32R, o_gh)
    wp_l, _ = place("wp_l", [P, 2, KT, P], F32R, o_gl)
    HOLE = W0 + 8192
    conv_acc, _ = place("conv_acc", [P, 2, S], F32, HOLE)
    rope, _ = place("rope", [P, 2, S], F32, HOLE)
    memX, _ = place("memX", [P, KT, M], F32, HOLE)
    Z0 = o_gl + 8192
    xbc, _ = place("xbc", [P, KT, S], F32, Z0)
    zy, _ = place("zy", [P, 4, S], F32, Z0 + 32768)
    vo, _ = place("vo", [P, 4, S], F32, Z0 + 49152)
    craw, _ = place("craw", [P, S + 8], F32, Z0 + 65536)
    o_small = Z0 + 65536 + 4 * (S + 8)
    small = []
    for name in ("dt_raw", "dt", "da", "cum", "w_state", "dt_tmp"):
        small.append(place(name, [P, TC, 16], F32, o_small)[0])
        o_small += 512
    dt_raw, dt, da, cum, w_state, dt_tmp = small
    w_dtg = dt_tmp
    etot, _ = place("etot", [P, TC, 16], F32, o_small)
    assert o_small + 512 <= nc.sbuf_usable_end, (o_small, nc.sbuf_usable_end)
    H0 = [XH0]

    def inH(name, shape, dt_=F32):
        t, o = place(name, shape, dt_, H0[0])
        H0[0] = o + -(-int(np.prod(shape[1:])) * 4 // 32) * 32
        assert H0[0] <= XH0 + 65536, name
        return t

    stage = inH("stage", [P, 2, KT, P])
    a_c = inH("a_c", [P, 2, 16])
    xs_n = inH("xs_n", [P, 2, NH, HD])
    b_n = inH("b_n", [P, 2, 2, P])
    xw = inH("xw", [P, 2, NH, HD])
    xdt = inH("xdt", [P, 2, 2, NH, HD])
    arg1 = [inH("arg1_0", [P, NH, P]), place("arg1_1", [P, NH, P], F32, W0)[0]]
    arg2 = [inH("arg2_0", [P, NH, P]), place("arg2_1", [P, NH, P], F32, W0 + 4096)[0]]
    ecum = [inH("ecum0", [P, 2, NH, P]),
            place("ecum1", [P, 2, NH, P], F32, HOLE)[0]]
    cb = inH("cb", [P, 2, 2, P])
    carry = inH("carry", [P, 2, NH * HD])
    pbc = inH("pbc", [P, 2, NH * HD])
    prev_b, _ = place("prev_b", [P, TC, NH * HD], F32, o_gh)
    tmps, _ = place("tmps", [P, 4, P], F32, Z0 + 65536)
    H0[0] = XH0
    q_h, q_l = (inH(n, [P, 2, S], F32R) for n in ("q_h", "q_l"))
    k_h, _ = place("k_h", [P, AH, S], F32R, o_gh)
    v_h, v_l = (inH(n, [P, KT, P], F32R) for n in ("v_h", "v_l"))
    pr = inH("pr", [P, 2, 2, S])
    att = inH("att", [P, 2, S])
    stat = inH("stat", [P, 2, 8, 2])
    lam = inH("lam", [P, 8])
    lam_t = inH("lam_t", [P, 2, HD])
    diag = inH("diag", [P, 2, P])
    aT_h, o_ = place("aT_h", [P, KT, HALF], F32R, Z0)
    aT_l, _ = place("aT_l", [P, KT, HALF], F32R, Z0 + 16384)
    rg, _ = place("rg", [P, 3, 48], F32, Z0 + 65536)
    g_out, _ = place("g_out", [P, 16], F32, Z0 + 65536 + 1024)
    qx, _ = place("qx", [P, KT, S], F32, Z0)
    kv, _ = place("kv", [P, 16, M], F32, Z0 + 32768)
    mem_h, _ = place("mem_h", [P, KT, M], F32R, Z0 + 49152)
    mem_l, _ = place("mem_l", [P, KT, M], F32R, Z0 + 57344)
    RM, _ = place("RM", [P, M], F32, Z0 + 65536 + 2048)
    rm, _ = place("rm", [P, 3, 2], F32, Z0 + 65536 + 3072)
    H0[0] = XH0
    cq_h, cq_l = (inH(n, [P, 2, 2, HALF], F32R) for n in ("cq_h", "cq_l"))
    ck_h, _ = place("ck_h", [P, 8, M], F32R, Z0 + 49152)
    ck_l, _ = place("ck_l", [P, 8, M], F32R, Z0 + 57344)
    cv_h, cv_l = (inH(n, [P, 2, M], F32R) for n in ("cv_h", "cv_l"))
    cp = inH("cp", [P, 2, 4, M])
    cpT_h, cpT_l = (inH(n, [P, 2, 2, HALF], F32R) for n in ("cpT_h", "cpT_l"))
    cstat = inH("cstat", [P, 2, 4, 4])
    gsq, _ = place("gsq", [P, KT, S], F32, Z0)
    sq_m, _ = place("sq_m", [P, 2, S], F32, Z0)
    ssum_m, _ = place("ssum_m", [P, S], F32, Z0 + 8192)

    ident = cst[:, IDENT:IDENT + P]
    ones = cst[:, ONES:ONES + P]
    trif = cst[:, TRIF:TRIF + P]
    trib = cst[:, TRIB:TRIB + P]
    x_spill = nc.dram_tensor("x_spill", (P, KT, S), F32, kind="Internal").ap()

    with ctx:
        PS = ctx.enter_context(nc.psum_tensor("PS", [P, 8, HALF], F32))
        sems = {}

        def sem(name):
            if name not in sems:
                sems[name] = ctx.enter_context(nc.semaphore(name))
            return sems[name]

        s_par, s_cst, s_wdt, s_rope, s_mem = (sem(n) for n in ("s_par", "s_cst", "s_wdt", "s_rope", "s_mem"))
        s_x = [sem(f"s_x{i}") for i in range(4)]
        s_gu = [sem(f"s_gu{i}") for i in range(2)]
        s_wd = [sem(f"s_wd{i}") for i in range(2)]
        s_wp = [sem(f"s_wp{i}") for i in range(2)]
        s_spill, s_out = sem("s_spill"), sem("s_out")
        s_back = [sem(f"s_back{i}") for i in range(4)]
        gu_hi, gu_lo, gu_used, wd_hi, wd_lo = (sem(n) for n in ("gu_hi", "gu_lo", "gu_used", "wd_hi", "wd_lo"))
        unit_done, unit_free, tg_done, silu_done, ta_done = (sem(n) for n in ("unit_done", "unit_free", "tg_done", "silu_done", "ta_done"))
        hid_hi, hid_lo, down_done = (sem(n) for n in ("hid_hi", "hid_lo", "down_done"))
        x_done, x_hi, x_lo = (sem(n) for n in ("x_done", "x_hi", "x_lo"))
        sq_done, sq_added = sem("sq_done"), sem("sq_added")
        rs_done, rs_inv, rn_done, rb_done, r_ready = (sem(n) for n in ("rs_done", "rs_inv", "rn_done", "rb_done", "r_ready"))
        wp_hi, wp_lo, blk_done, blk_free = (sem(n) for n in ("wp_hi", "wp_lo", "blk_done", "blk_free"))
        conv_done, conv_silu, swap_done, qk_ready = (sem(n) for n in ("conv_done", "conv_silu", "swap_done", "qk_ready"))
        wdt_done, dt_done, dt_out = (sem(n) for n in ("wdt_done", "dt_done", "dt_out"))
        sp_step, sp_act, cum_done = (sem(n) for n in ("sp_step", "sp_act", "cum_done"))
        pb_mul = sem("pb_mul")
        stage_done, nat_tr, nat_done, xw_done, st_done, pb_done = (sem(n) for n in ("stage_done", "nat_tr", "nat_done", "xw_done", "st_done", "pb_done"))
        rows_done, arg_done, e_done, ecum_done, xdt_done, cdec_done = (sem(n) for n in ("rows_done", "arg_done", "e_done", "ecum_done", "xdt_done", "cdec_done"))
        cb_done, cb_used, m_done, y_done, y_out, carry_done = (sem(n) for n in ("cb_done", "cb_used", "m_done", "y_done", "y_out", "carry_done"))
        stage2, nat2_tr, nat2_done, xw2_done, st2_done = (sem(n) for n in ("stage2", "nat2_tr", "nat2_done", "xw2_done", "st2_done"))
        lam_sum, lam_exp = sem("lam_sum"), sem("lam_exp")
        q_hi, q_lo, k_hi, k_lo, v_back, v_tr, v_hi, v_lo = (sem(n) for n in ("q_hi", "q_lo", "k_hi", "k_lo", "v_back", "v_tr", "v_hi", "v_lo"))
        sc_done, nm_done, exp_done, comb_done, scaled, max_done, inv_done, ratio_done, at_tr, at_hi, at_lo, pv_done, o_done = (sem(n) for n in (
            "sc_done", "nm_done", "exp_done", "comb_done", "scaled", "max_done", "inv_done", "ratio_done", "at_tr", "at_hi", "at_lo", "pv_done", "o_done"))
        gsq_done, gsum_done, grow_done, ginv_done, groot_done, gs_done, gs_free = (sem(n) for n in (
            "gsq_done", "gsum_done", "grow_done", "ginv_done", "groot_done", "gs_done", "gs_free"))
        g_done = sem("g_done")
        msq_done, msum_done, mrow_done, minv_done, mroot_done, mspread_done, mr_done, mem_hi, mem_lo = (sem(n) for n in (
            "msq_done", "msum_done", "mrow_done", "minv_done", "mroot_done", "mspread_done", "mr_done", "mem_hi", "mem_lo"))
        ck_hi, ck_lo, cq_hi, cq_lo, cv_back, cv_tr, cv_hi, cv_lo = (sem(n) for n in ("ck_hi", "ck_lo", "cq_hi", "cq_lo", "cv_back", "cv_tr", "cv_hi", "cv_lo"))
        cmax_done, cinv_done, zeros_done = sem("cmax_done"), sem("cinv_done"), sem("zeros_done")
        first_a = sem("first_a")
        cs_done, cnm_done, cexp_done, cnorm_done, cp_tr, cp_hi, cp_lo, cpv_done, co_done = (sem(n) for n in (
            "cs_done", "cnm_done", "cexp_done", "cnorm_done", "cp_tr", "cp_hi", "cp_lo", "cpv_done", "co_done"))
        fin_done = sem("fin_done")
        dve_own, pool_own = sem("dve_own"), sem("pool_own")

        block = ctx.enter_context(nc.Block())

        def squares_of(n):
            return (sq_m, ssum_m) if n in (2, 3) else (sq, ssum)

        def chunk(c):
            return bass.ds(c * P, P) if not isinstance(c, int) else slice(c * P, (c + 1) * P)

        def in_groups(i, j):
            return not isinstance(i, int) or 0 <= 2 * i + j < 2 * AH

        def groups(eng, step):
            for j in range(2):
                step(0, j)
            with eng.Fori(1, AH - 1) as i:
                for j in range(2):
                    step(i, j)
            for j in range(4):
                step(AH - 1, j)

        def one(j):
            return bass.ds(j, 1)

        def after(eng, sem_, i, per, n):
            if not isinstance(i, int) or i * per + n > 0:
                eng.wait_ge(sem_, i * per + n)

        def heads_in_turn(step, split_v):
            for s in range(3):
                step(0, s)
            split_v(0)

            def body(h, last=False):
                for s in range(3, TC - 1):
                    step(h, s, next_head=None if last else h + 1)
                step(h, TC - 1, following=None if last else h + 1)
                for s in range(TC, TC + 3):
                    if not last:
                        step(h + 1, s - TC, (h, s))
                    else:
                        step(None, None, (h, s))
                if not last:
                    split_v(h + 1)

            return body

        @block.sync
        def _(sp):
            sp.dma_start(par[:], par_d).then_inc(s_par, 16)
            sp.dma_start(wgu_raw[:, 0], wgu1[0]).then_inc(s_gu[0], 16)
            for q in range(4):
                sp.dma_start(X[:, 2 * q:2 * q + 2], xT[:, 2 * q:2 * q + 2]).then_inc(s_x[q], 16)
            sp.dma_start(cst[:], cst_d).then_inc(s_cst, 16)

            def ffn_loads(f, wgu, wd):
                c0 = f * FC
                if f:
                    sp.wait_ge(wp_lo, B_END)
                for c in range(1 - f, 2):
                    sp.dma_start(wgu_raw[:, c], wgu[c]).then_inc(s_gu[c], 16)
                if f:
                    sp.wait_ge(rs_done, 4)
                for c in range(2):
                    sp.dma_start(wd_raw[:, c], wd[c]).then_inc(s_wd[c], 16)
                with sp.Fori(1, PAIRS) as i:
                    for c in range(2):
                        sp.wait_ge(gu_lo, i * 8 + (4 * (c0 + c - 1)))
                        sp.dma_start(wgu_raw[:, c], wgu[one(i * 2 + c)].rearrange("o p k w n -> (o p) k w n")).then_inc(s_gu[c], 16)
                        sp.wait_ge(wd_lo, i * 2 + (c0 + c - 1))
                        sp.dma_start(wd_raw[:, c], wd[one(i * 2 + c)].rearrange("o p n -> (o p) n")).then_inc(s_wd[c], 16)

            def projection_loads(w, b0, b1):
                with sp.Fori(0, (b1 - b0) // 2) as i:
                    for j in range(2):
                        sp.wait_ge(wp_lo, i * 2 + (b0 + j - 1))
                        sp.dma_start(wp_raw[:, j], w[one(i * 2 + j)].rearrange("o p k n -> (o p) k n")).then_inc(s_wp[j], 16)

            ffn_loads(0, wgu1, wd1)
            sp.dma_start(dt_raw[:], w_dt).then_inc(s_wdt, 16)
            sp.wait_ge(gu_lo, 4 * (FC - 1))
            for j in range(2):
                sp.dma_start(wp_raw[:, j], w_in[j]).then_inc(s_wp[j], 16)
            sp.wait_ge(x_done, XB[1])
            sp.dma_start(x_spill, X[:]).then_inc(s_spill, 16)

            def w_in_loads(i0, i1):
                with sp.Fori(i0, i1) as i:
                    for j in range(2):
                        sp.wait_ge(wp_lo, i * 2 + (j - 1))
                        sp.dma_start(wp_raw[:, j], w_in[one(i * 2 + j)].rearrange("o p k n -> (o p) k n")).then_inc(s_wp[j], 16)

            w_in_loads(1, B_QK // 2)
            sp.wait_ge(conv_silu, B_V + 1)
            sp.dma_start(rope[:], rope_d).then_inc(s_rope, 16)
            w_in_loads(B_QK // 2, B_OUT // 2)

            sp.wait_ge(y_out, TC + 1)
            sp.dma_start(memX[:], memT).then_inc(s_mem, 16)
            sp.wait_ge(pv_done, 4 * AH + 1)
            for q in range(4):
                sp.dma_start(X[:, 2 * q:2 * q + 2], x_spill[:, 2 * q:2 * q + 2]).then_inc(s_back[q], 16)
            projection_loads(w_out, B_OUT, B_KV)
            projection_loads(w_kv, B_KV, B_Q)
            projection_loads(w_q, B_Q, B_O)
            projection_loads(w_o, B_O, B_END)
            ffn_loads(1, wgu2, wd2)
            for k in range(KT):
                sp.wait_ge(fin_done, k + 1)
                sp.dma_start(out[:, k], X[:, k]).then_inc(s_out, 16)
            sp.wait_ge(s_out, 16 * KT)

        @block.scalar
        def _(act):
            def high_weights(p, gain, src):
                for k in range(KT):
                    last = nc.scalar.activation(wp_h[:, p, k], wp_raw[:, p, k], ACT.Copy, scale=src[:, gain + k:gain + k + 1])
                    if k % 4 == 3:
                        last.then_inc(wp_hi, 1)

            def split_weights(i, b, gain, src, hook=None):
                act.wait_ge(s_wp[b % 2], i * 16 + 16 * (b // 2 + 1))
                if hook:
                    hook()
                elif b > 1:
                    act.wait_ge(blk_done, i * 2 + (b - 1))
                elif not isinstance(i, int):
                    act.wait_ge(blk_done, i * 2 + b - 1)
                high_weights(b % 2, gain, src)

            def split_x(e, n, x_ready, both=True):
                sq_, _ = squares_of(n)

                def high(k):
                    x_ready(k)
                    nc.scalar.activation(XH[:, k], X[:, k], ACT.Copy).then_inc(x_hi, 1)

                def square(k):
                    if k >= 2 or n > 0:
                        act.wait_ge(sq_added, KT * n + k - 1)
                    nc.scalar.activation(sq_[:, k % 2], X[:, k], ACT.Square).then_inc(sq_done, 1)

                if n == 0:
                    for k in range(KT):
                        high(k)
                    for k in range(KT):
                        square(k)
                else:
                    for k in range(KT):
                        if both:
                            high(k)
                        else:
                            x_ready(k)
                        square(k)

            def split_gu_first(pieces):
                act.wait_ge(s_gu[0], 16 * (PAIRS + 1))
                for q in pieces:
                    act.wait_ge(blk_done, B_END - 1 if q < 2 else B_END)
                    for k in range(2 * q, 2 * q + 2):
                        last = nc.scalar.activation(wgu_h[:, k], wgu_raw[:, 0, k], ACT.Copy, scale=par[:, G_FFN2 + k:G_FFN2 + k + 1])
                    last.then_inc(gu_hi, 1)

            def root(n):
                act.wait_ge(rs_inv, n + 1)
                nc.scalar.activation(rn[:, 2, 0:TC], rn[:, 1, 0:TC], ACT.Sqrt).then_inc(rn_done, 1)

            def ffn(f, n, gain, before, after):
                c0, u0 = f * FC, 2 * f * FC

                def split_gu(i, c, pieces=range(4), first=False):
                    act.wait_ge(s_gu[c % 2], (i + c // 2) * 16 + 16 * (PAIRS * f + 1))
                    for q in pieces:
                        if not first:
                            if q < 3:
                                act.wait_ge(gu_used, i * 6 + (3 * (c0 + c - 1) + q + 1))
                            else:
                                act.wait_ge(unit_done, i * 4 + 2 * (c0 + c))
                        for k in range(2 * q, 2 * q + 2):
                            last = nc.scalar.activation(wgu_h[:, k], wgu_raw[:, c % 2, k], ACT.Copy,
                                                        scale=par[:, gain + k:gain + k + 1])
                        last.then_inc(gu_hi, 1)

                def split_wd(i, c, first=False):
                    act.wait_ge(s_wd[c], i * 16 + 16 * (PAIRS * f + 1))
                    if not first:
                        act.wait_ge(down_done, i * KT + KT * PAIRS * f)
                    nc.scalar.activation(wd_h[:, c], wd_raw[:, c], ACT.Copy).then_inc(wd_hi, 1)

                def unit(i, u):
                    act.wait_ge(tg_done, i * 4 + (u0 + u + 1))
                    nc.scalar.activation(tsl[:, u % 2], tg[:, u % 2], ACT.Silu).then_inc(silu_done, 1)
                    act.wait_ge(ta_done, i * 4 + (u0 + u + 1))
                    nc.scalar.activation(hid_h[:, u // 2, u % 2 * HALF:(u % 2 + 1) * HALF], ta[:, u % 2],
                                         ACT.Copy).then_inc(hid_hi, 1)

                if f:
                    split_gu_first(range(2, 4))
                else:
                    split_gu(0, 0, first=True)
                before()
                root(n)

                def pair(i, last=False, first=False):
                    unit(i, 0)
                    split_wd(i, 0, first)
                    split_wd(i, 1, first)
                    split_gu(i, 1)
                    unit(i, 1)
                    unit(i, 2)
                    if not last:
                        split_gu(i, 2, range(3))
                    unit(i, 3)
                    if not last:
                        split_gu(i, 2, range(3, 4))

                pair(0, first=f == 0)
                with act.Fori(1, PAIRS - 1) as i:
                    pair(i)
                pair(PAIRS - 1, last=True)
                after()

            def x_loaded(k):
                act.wait_ge(s_x[k // 2], 16)

            def x_written(n):
                def wait(k):
                    act.wait_ge(x_done, XB[n] - KT + k + 1)
                    if k == 0 and n == 1:
                        act.wait_ge(unit_done, 2 * FC)
                    if k == 0 and n == 3:
                        act.wait_ge(blk_done, B_END)
                return wait

            def to_mixer():
                def ready():
                    act.wait_ge(unit_done, 2 * FC)
                split_weights(0, 0, G_MIX, par, ready)
                split_x(1, 1, x_written(1))
                root(1)

            act.wait_ge(s_par, 16)
            ffn(0, 0, G_FFN1, lambda: split_x(0, 0, x_loaded), to_mixer)

            def conv_block(i, b, dst, j):
                if b < B_Z:
                    act.wait_ge(conv_done, i * 2 + b + 2)
                    nc.scalar.activation(dst[:, one(i * 2 + j)], conv_acc[:, b % 2:b % 2 + 1], ACT.Silu,
                                         bias=par[:, one(i * 2 + (CONVB + j))]).then_inc(conv_silu, 1)
                else:
                    act.wait_ge(blk_free, i * 2 + b + 1)
                    nc.scalar.activation(dst[:, one(i * 2 + j)], conv_acc[:, b % 2:b % 2 + 1], ACT.Silu).then_inc(conv_silu, 1)

            act.wait_ge(s_wp[1], 16)
            high_weights(1, G_MIX, par)
            with act.Fori(0, (B_Z - B_XBC) // 2) as i:
                for j in range(2):
                    split_weights(i, j + 2, G_MIX, par)
                    conv_block(i, j, xbc, j)
            act.wait_ge(sp_step, 1)
            nc.scalar.activation(w_state[:], etot[:], ACT.Exp, scale=-1.0).then_inc(sp_act, 1)
            act.wait_ge(sp_step, 2)
            nc.scalar.activation(cum[:], etot[:], ACT.Ln).then_inc(sp_act, 1)
            act.wait_ge(sp_act, 2)
            nc.scalar.activation(rn[:, 0, :], par[:, ALOG:ALOG + 16], ACT.Exp).then_inc(sp_act, 1)
            with act.Fori(0, (B_V - B_Z) // 2) as i:
                for j in range(2):
                    split_weights(i, B_Z + j + 2, G_MIX, par)
                    conv_block(i, B_Z + j, zy, j)
            act.wait_ge(sp_step, 3)
            nc.scalar.activation(w_state[:], dt_tmp[:], ACT.Exp).then_inc(sp_act, 1)
            nc.scalar.activation(etot[:], PS[:, 6, 0:P].rearrange("p (c h) -> p c h", c=TC), ACT.Exp).then_inc(sp_act, 1)
            with act.Fori(0, (B_OUT - 2 - B_V) // 2) as i:
                for j in range(2):
                    split_weights(i, B_V + j + 2, G_MIX, par)

            def natural(w, p):
                nc.scalar.activation(xs_n[:, p], PS[:, 4].rearrange("p (h d) -> p h d", h=NH), ACT.Copy)
                nc.scalar.activation(b_n[:, p], PS[:, 5, 0:2 * P].rearrange("p (g n) -> p g n", g=2), ACT.Copy).then_inc(w, 1)

            def fix(i, r):
                act_c = (TC - 1 - r) if isinstance(i, int) else i * -2 + (TC - 1 - r)
                nc.scalar.activation(stage[:, r % 2, 0:6], xbc[:, 0:6, chunk(act_c)], ACT.Copy).then_inc(stage_done, 1)

            def turned(i, r):
                act.wait_ge(nat_tr, i * 2 + (r + 1))
                if r >= 2 or not isinstance(i, int):
                    after(act, xw_done, i, 2, max(r - 1, 0) + 1)
                    after(act, st_done, i, 2, max(r - 1, 0) + 1)
                natural(nat_done, r % 2)

            act.wait_ge(blk_done, B_OUT)
            fix(0, 0)
            fix(0, 1)
            with act.Fori(0, 2) as i:
                for r in range(2):
                    turned(i, r)
                    fix(i, r + 2)
            turned(0, 4)
            fix(0, 6)
            turned(0, 5)
            turned(0, 6)

            def front(i, c):
                act.wait_ge(nat2_tr, i * 2 + (c + 1))
                if c >= 2 or not isinstance(i, int):
                    act.wait_ge(st2_done, i * 2 + c)
                    act.wait_ge(xdt_done, i * 2 + c)
                elif c == 0:
                    act.wait_ge(st_done, TC)
                if c == 0 and isinstance(i, int):
                    act.wait_ge(pb_done, TC)
                else:
                    act.wait_ge(y_done, i * 2 + c)
                nc.scalar.activation(pbc[:, c % 2:c % 2 + 1], prev_b[:, one(i * 2 + c)], ACT.Copy)
                natural(nat2_done, c % 2)

            def back(i, c):
                act.wait_ge(arg_done, i * 2 + (c + 1))
                nc.scalar.activation(arg1[c % 2][:], arg1[c % 2][:], ACT.Exp).then_inc(e_done, 1)
                for d in range(2):
                    last = nc.scalar.activation(ecum[c % 2][:, d], PS[:, 2 * d:2 * d + 2].rearrange("p a (h l) -> p (a h) l", l=P), ACT.Exp)
                last.then_inc(ecum_done, 1)

            front(0, 0)
            with act.Fori(0, TC // 2 - 1) as i:
                for c in range(2):
                    back(i, c)
                    front(i, c + 1)
            back(0, TC - 2)
            front(0, TC - 1)
            back(0, TC - 1)


            def split_q(h):
                after(act, sc_done, h, 16, 0)
                for t in range(2):
                    r = slice(t * HD, (t + 1) * HD)
                    nc.scalar.activation(q_h[r, t], X[r, one(h)].rearrange("p o s -> p (o s)"), ACT.Copy).then_inc(q_hi, 1)

            def split_k(h):
                nc.scalar.activation(k_h[:, one(h)], X[:, one(h + AH)], ACT.Copy).then_inc(k_hi, 1)

            def split_v(h):
                after(act, pv_done, h, 4, 1)
                nc.scalar.activation(v_h[:], vo[:, one(h)].rearrange("p o (k e) -> p (o k) e", e=P), ACT.Copy).then_inc(v_hi, 1)

            def exps(h, s, maps):
                after(act, comb_done, h, TC, s - 1)
                for t in maps:
                    act.wait_ge(nm_done, h * 16 + (2 * s + t + 1))
                    nc.scalar.activation(pr[:, s % 2, t], PS[:, 2 * t:2 * t + 2].rearrange("p a b -> p (a b)"), ACT.Exp,
                                         bias=stat[:, s % 2, 2 + t, 0:1], scale=0.125,
                                         accum_out=stat[:, s % 2, 4 + t, 0:1]).then_inc(exp_done, 1)

            def scale(h, s):
                act.wait_ge(ratio_done, h * TC + (s + 1))
                nc.scalar.activation(pr[:, s % 2, 1], pr[:, s % 2, 1], ACT.Copy, scale=stat[:, s % 2, 7, 1:2]).then_inc(scaled, 1)

            def high(h, q):
                act.wait_ge(at_tr, h * TC + (q + 1))
                after(act, pv_done, h, 4, (q // 2 - 1 if q != 1 else 0) + 1)
                nc.scalar.activation(aT_h[:, :, q % 4 * P:(q % 4 + 1) * P],
                                     PS[:, 4:6].rearrange("p a (k q) -> p (a k) q", q=P), ACT.Copy).then_inc(at_hi, 1)

            def step(h, s, before=None, following=None, next_head=None):
                for h_, s_ in ((h, s), before or (None, None)):
                    if h_ is not None and 1 <= s_ <= TC:
                        scale(h_, s_ - 1)
                if s == TC - 3 and next_head is not None:
                    split_k(next_head)
                if following is not None:
                    split_q(following)
                if h is not None:
                    exps(h, s, (0,))
                for h_, s_ in ((h, s), before or (None, None)):
                    if h_ is not None and 2 <= s_ <= TC + 1:
                        high(h_, s_ - 2)
                if h is not None:
                    exps(h, s, (1,))

            split_k(0)
            for w in (st2_done, xdt_done, cdec_done, cb_done):
                act.wait_ge(w, TC + 1)
            split_q(0)
            act.wait_ge(lam_sum, 1)
            nc.scalar.activation(lam[:, 2:4], lam[:, 0:2], ACT.Exp).then_inc(lam_exp, 1)
            body = heads_in_turn(step, split_v)
            with act.Fori(0, AH - 1) as h:
                body(h)
            body(AH - 1, last=True)

            act.wait_ge(pv_done, 4 * AH + 1)
            for k in range(KT):
                if k >= 4:
                    act.wait_ge(o_done, 4 * (k - 3) + 1)
                src = zy[:, k] if k < 4 else vo[:, k - 4]
                nc.scalar.activation(gsq[:, k], src, ACT.Square).then_inc(gsq_done, 1)
            act.wait_ge(ginv_done, 1)
            nc.scalar.activation(rg[:, 2], rg[:, 1], ACT.Sqrt).then_inc(groot_done, 1)
            act.wait_ge(g_done, 1)
            split_weights(0, B_OUT, 0, g_out)
            for k in range(KT):
                act.wait_ge(gs_free, k + 1)
                src = zy[:, k] if k < 4 else vo[:, k - 4]
                nc.scalar.activation(XH[:, k], src, ACT.Copy).then_inc(x_hi, 1)
            act.wait_ge(s_mem, 16)
            act.wait_ge(x_lo, 3 * KT)
            nc.scalar.activation(mem_h[:], memX[:], ACT.Copy).then_inc(mem_hi, 1)
            nc.scalar.activation(qx[:, 4:6].rearrange("p a b -> p (a b)"), memX[:].rearrange("p k m -> p (k m)"), ACT.Square).then_inc(msq_done, 1)
            act.wait_ge(minv_done, 1)
            nc.scalar.activation(rm[:, 2], rm[:, 1], ACT.Sqrt).then_inc(mroot_done, 1)

            def square_loop(n, b0, b1, gain, src, following):
                def square(i, j):
                    act.wait_ge(x_done, i * 2 + (XB[n] - KT + j + 1))
                    act.wait_ge(sq_added, i * 2 + (KT * n + j - 1))
                    nc.scalar.activation(sq_m[:, j:j + 1], X[:, one(i * 2 + j)], ACT.Square).then_inc(sq_done, 1)
                with act.Fori(0, (b1 - b0) // 2 - 1) as i:
                    for j in range(2):
                        split_weights(i, b0 + j + 1, gain, src)
                        square(i, j)
                split_weights(0, b1 - 1, gain, src)
                square(KT // 2 - 1, 0)
                following()
                square(KT // 2 - 1, 1)

            square_loop(2, B_OUT, B_KV, 0, g_out, lambda: split_weights(0, B_KV, G_MEM, par))
            split_weights(0, B_KV + 1, G_MEM, par)
            root(2)
            with act.Fori(0, (B_Q - B_KV) // 2 - 1) as i:
                for j in range(2):
                    split_weights(i, B_KV + j + 2, G_MEM, par)
                nc.scalar.activation(XH[:, one(i)], X[:, one(i)], ACT.Copy).then_inc(x_hi, 1)
            nc.scalar.activation(XH[:, KT - 1], X[:, KT - 1], ACT.Copy).then_inc(x_hi, 1)
            split_weights(0, B_Q, G_XQ, par)
            act.wait_ge(cv_tr, 1)
            nc.scalar.activation(kv[:, 8:12], PS[:, 4:6].rearrange("p h (m e) -> p (h m) e", m=2), ACT.Copy).then_inc(cv_back, 1)
            nc.scalar.activation(ck_h[:], kv[:, 0:8], ACT.Copy).then_inc(ck_hi, 1)
            with act.Fori(0, (B_O - B_Q) // 2 - 1) as i:
                for j in range(2):
                    split_weights(i, B_Q + j + 1, G_XQ, par)
            split_weights(0, B_O - 1, G_XQ, par)

            act.wait_ge(blk_free, B_O - KT)
            act.wait_ge(cv_back, 2)

            def split_q(i, j):
                h, p = i + j // 2, j % 2
                after(act, cs_done, i, 2, j - 1)
                nc.scalar.activation(cq_h[:, p], qx[:, bass.ds(h * 2, 2), p * HALF:(p + 1) * HALF], ACT.Copy).then_inc(cq_hi, 1)

            def split_v(i, j):
                after(act, cpv_done, i, 2, j + 1)
                nc.scalar.activation(cv_h[:], kv[:, bass.ds((i + j // 2) * 2 + 8, 2)], ACT.Copy).then_inc(cv_hi, 1)

            def exps(i, j):
                p = j % 2
                act.wait_ge(cnm_done, i * 2 + (j + 1))
                after(act, cp_tr, i, 2, j - 1)
                for t in range(4):
                    last = nc.scalar.activation(cp[:, p, t], PS[:, 2 * p + t // 2, t % 2 * M:(t % 2 + 1) * M], ACT.Exp, bias=cstat[:, p, 1, t:t + 1],
                                                scale=0.0625, accum_out=cstat[:, p, 2, t:t + 1])
                last.then_inc(cexp_done, 1)

            def high(i, j):
                act.wait_ge(cp_tr, i * 2 + (j + 1))
                after(act, cpv_done, i, 2, j)
                nc.scalar.activation(cpT_h[:, j % 2], PS[:, 4:6], ACT.Copy).then_inc(cp_hi, 1)

            def step(i, j):
                if in_groups(i, j + 1):
                    split_q(i, j + 1)
                if in_groups(i, j):
                    exps(i, j)
                if in_groups(i, j - 1):
                    high(i, j - 1)
                if j == 1 and in_groups(i, 0):
                    split_v(i, 0)

            split_q(0, 0)
            groups(act, step)
            split_weights(0, B_O, 8, g_out)
            for k in range(KT):
                if k == 0:
                    act.wait_ge(cpv_done, 2 * AH + 1)
                act.wait_ge(co_done, 2 * (k // 2 + 1) + 1)
                nc.scalar.activation(XH[:, k], qx[:, k], ACT.Copy).then_inc(x_hi, 1)
            square_loop(3, B_O, B_END, 8, g_out, lambda: split_gu_first(range(2)))

            def to_ffn2():
                for k in range(KT):
                    nc.scalar.activation(XH[:, k], X[:, k], ACT.Copy).then_inc(x_hi, 1)

            def to_end():
                for k in range(KT):
                    act.wait_ge(x_done, XB[4] - KT + k + 1)
                    act.wait_ge(sq_added, KT * 4 + k - 1)
                    nc.scalar.activation(sq[:, k % 2], X[:, k], ACT.Square).then_inc(sq_done, 1)
                root(4)

            ffn(1, 3, G_FFN2, to_ffn2, to_end)

        @block.gpsimd
        def _(pool):
            own = Steps(pool, pool_own)

            def sum_squares(n):
                sq_, ssum_ = squares_of(n)
                for k in range(KT):
                    pool.wait_ge(sq_done, KT * n + k + 1)
                    if k == 0:
                        if n > 0:
                            pool.wait_ge(rs_done, n)
                        last = nc.gpsimd.tensor_copy(ssum_[:], sq_[:, 0])
                    else:
                        last = nc.gpsimd.tensor_tensor(ssum_[:], ssum_[:], sq_[:, k % 2], ALU.add)
                    last.then_inc(sq_added, 1)
                    pool.wait_ge(sq_added, KT * n + k + 1)

            sum_squares(1)

            pool.wait_ge(sp_step, 4)
            pool.wait_ge(blk_done, B_OUT)
            pool.tensor_copy(a_c[:, 0], da[:, 0]).then_inc(first_a, 1)

            def weigh(i, r):
                c = (TC - 1 - r) if isinstance(i, int) else i * -2 + (TC - 1 - r)
                if r >= 2 or not isinstance(i, int):
                    after(pool, st_done, i, 2, max(r - 1, 0) + 1)
                pool.wait_ge(nat_done, i * 2 + (r + 1))
                pool.tensor_tensor(xw[:, r % 2], xs_n[:, r % 2], w_state[:, one(c), 8:16].rearrange("p o h -> p (o h)").unsqueeze(2).to_broadcast([P, NH, HD]),
                                   ALU.mult).then_inc(xw_done, 1)

            with pool.Fori(0, 3) as i:
                for r in range(2):
                    weigh(i, r)
            weigh(0, 6)

            def front(i, c):
                p = c % 2
                if c >= 2 or not isinstance(i, int):
                    pool.wait_ge(cb_done, i * 2 + c)
                    pool.wait_ge(cdec_done, i * 2 + c)
                elif c == 0:
                    pool.wait_ge(nat_tr, TC - 1)
                if c >= 1 or not isinstance(i, int):
                    pool.tensor_copy(a_c[:, p:p + 1], da[:, one(i * 2 + c)])
                pool.tensor_copy(stage[:, p], xbc[:, :, chunk(i * 2 + c)]).then_inc(stage2, 1)

            def back(i, c):
                p = c % 2

                def per_head(t, d):
                    return t[:, one(i * 2 + c), 8 * d:8 * d + 8].rearrange("p o h -> p (o h)").unsqueeze(2).to_broadcast([P, NH, HD])
                pool.wait_ge(nat2_done, i * 2 + (c + 1))
                if isinstance(i, int) and c == 0:
                    pool.wait_ge(st_done, TC)
                else:
                    pool.wait_ge(st2_done, i * 2 + (c + 1))
                pool.tensor_tensor(xw[:, p], xs_n[:, p], per_head(w_state, 0), ALU.mult).then_inc(xw2_done, 1)
                for d in range(2):
                    last = pool.tensor_tensor(xdt[:, p, d], xs_n[:, p], per_head(dt, d), ALU.mult)
                last.then_inc(xdt_done, 1)
                pool.wait_ge(ecum_done, i * 2 + (c + 1))
                for d in range(2):
                    e = ecum[p][:, d].rearrange("p (g r) l -> p g r l", g=2)
                    last = pool.tensor_tensor(e, e, stage[:, p, 6:8].unsqueeze(2).to_broadcast([P, 2, 4, P]), ALU.mult)
                last.then_inc(cdec_done, 1)

            front(0, 0)
            with pool.Fori(0, TC // 2 - 1) as i:
                for c in range(2):
                    front(i, c + 1)
                    back(i, c)
            front(0, TC - 1)
            back(0, TC - 2)
            back(0, TC - 1)

            for w in (st2_done, xdt_done, cdec_done, cb_done):
                pool.wait_ge(w, TC + 1)
            for q_ in (q_h, q_l):
                for t in range(2):
                    last = pool.memset(q_[(1 - t) * HD:(2 - t) * HD, t].bitcast(F32), 0.0)
            last.then_inc(zeros_done, 1)

            def combine(h, s):
                after(pool, at_tr, h, TC, s - 1)
                pool.wait_ge(ratio_done, h * TC + (s + 1))
                pool.tensor_tensor(diag[:, s % 2], ident, stat[:, s % 2, 6, 0:1].to_broadcast([P, P]), ALU.mult)
                pool.wait_ge(scaled, h * TC + (s + 1))
                pool.tensor_tensor(att[:, s % 2], pr[:, s % 2, 1], pr[:, s % 2, 0], ALU.add).then_inc(comb_done, 1)

            def step(h, s, before=None, following=None, next_head=None):
                for h_, s_ in ((h, s), before or (None, None)):
                    if h_ is not None and 1 <= s_ <= TC:
                        combine(h_, s_ - 1)

            body = heads_in_turn(step, lambda h: None)
            with pool.Fori(0, AH - 1) as h:
                body(h)
            body(AH - 1, last=True)

            for g in range(2):
                pool.wait_ge(gsq_done, 2 * g + 2)
                pool.tensor_tensor(gsq[:, 2 * g], gsq[:, 2 * g], gsq[:, 2 * g + 1], ALU.add).then_inc(gsum_done, 1)
            pool.wait_ge(msq_done, 1)
            own.done(pool.tensor_tensor(qx[:, 4], qx[:, 4], qx[:, 5], ALU.add))
            own.done(pool.tensor_tensor(qx[:, 4, 0:HALF], qx[:, 4, 0:HALF], qx[:, 4, HALF:S], ALU.add))
            pool.tensor_tensor(qx[:, 4, 0:M], qx[:, 4, 0:M], qx[:, 4, M:2 * M], ALU.add).then_inc(msum_done, 1)
            sum_squares(2)
            sum_squares(3)
            sum_squares(4)

        @block.tensor
        def _(pe):
            def root_rows(n):
                _, ssum_ = squares_of(n)
                if n == 0:
                    pe.wait_ge(s_cst, 16)
                pe.wait_ge(sq_added, KT * (n + 1))
                for t in range(TC):
                    last = nc.tensor.matmul(PS[:, 6, t:t + 1], ssum_[:, t * P:(t + 1) * P],
                                            cst[:, INV1024:INV1024 + 1], start=True, stop=True)
                last.then_inc(rs_done, 1)

            def root_spread(n):
                pe.wait_ge(rn_done, n + 1)
                for t in range(TC):
                    last = nc.tensor.matmul(PS[:, 4 + t // 4, t % 4 * P:(t % 4 + 1) * P],
                                            rn[:, 2, t:t + 1].to_broadcast([P, P]), ident, start=True, stop=True)
                last.then_inc(rb_done, 1)

            def ffn(f, n, e):
                c0, u0 = f * FC, 2 * f * FC

                def gate_up(i, c, half, first, firstunit=False, rows_at=None):
                    u = 2 * c + half
                    if not first:
                        pe.wait_ge(unit_free, i * 4 + (u0 + u - 1))
                    bank = 2 * half
                    tok = slice(half * HALF, (half + 1) * HALF)
                    for k in range(KT):
                        if half == 0 and k % 2 == 0:
                            pe.wait_ge(gu_lo, i * 8 + (4 * (c0 + c) + k // 2 + 1))
                        if firstunit:
                            pe.wait_ge(x_lo, KT * e + k + 1)
                        if k == rows_at:
                            root_rows(n)
                        for w in range(2):
                            o = PS[:, bank + w]
                            nc.tensor.matmul(o, wgu_h[:, k, w], XH[:, k, tok], start=k == 0, stop=False)
                            nc.tensor.matmul(o, wgu_h[:, k, w], XL[:, k, tok], start=False, stop=False)
                            last = nc.tensor.matmul(o, wgu_l[:, k, w], XH[:, k, tok], start=False, stop=k == KT - 1)
                        if half == 1 and k in (1, 3, 5):
                            last.then_inc(gu_used, 1)
                    last.then_inc(unit_done, 1)

                def down(i, first):
                    def part(m, c, half):
                        o = PS[:, 4 + 2 * (m % 2) + half]
                        w, tok = slice(m * P, (m + 1) * P), slice(half * HALF, (half + 1) * HALF)
                        nc.tensor.matmul(o, wd_h[:, c, w], hid_h[:, c, tok], start=c == 0, stop=False)
                        nc.tensor.matmul(o, wd_h[:, c, w], hid_l[:, c, tok], start=False, stop=False)
                        return nc.tensor.matmul(o, wd_l[:, c, w], hid_h[:, c, tok], start=False, stop=c == 1)

                    def down_free(i, m):
                        pe.wait_ge(x_done, i * KT + (XB[n] + m - 1))

                    pe.wait_ge(wd_lo, i * 2 + (c0 + 2))
                    pe.wait_ge(hid_lo, i * 4 + (u0 + 2))
                    if first:
                        pe.wait_ge(r_ready, n + 1)
                    for m in range(2):
                        if not first:
                            down_free(i, m)
                        part(m, 0, 0)
                        part(m, 0, 1)
                    pe.wait_ge(hid_lo, i * 4 + (u0 + 3))
                    part(0, 1, 0)
                    part(1, 1, 0)
                    pe.wait_ge(hid_lo, i * 4 + (u0 + 4))
                    part(0, 1, 1).then_inc(down_done, 1)
                    part(1, 1, 1).then_inc(down_done, 1)
                    for m in range(2, KT):
                        down_free(i, m)
                        for c in range(2):
                            for half in range(2):
                                last = part(m, c, half)
                        last.then_inc(down_done, 1)

                def pair(i, first=False):
                    gate_up(i, 0, 0, first, firstunit=first, rows_at=KT // 2 if first and f else None)
                    if first and f:
                        root_spread(n)
                    gate_up(i, 0, 1, first, rows_at=6 if first and not f else None)
                    if first and not f:
                        root_spread(n)
                    gate_up(i, 1, 0, False)
                    gate_up(i, 1, 1, False)
                    down(i, first)

                pair(0, first=True)
                with pe.Fori(1, PAIRS) as i:
                    pair(i)

            def proj(i, b, hi=XH, lo=XL, n_tok=S, free=None, e=None, n=None):
                pe.wait_ge(wp_lo, i * 2 + (b + 1))
                if free:
                    pe.wait_ge(free[0], i * 2 + (b + free[1] - 1))
                w = min(n_tok, HALF)
                for k in range(KT):
                    if e is not None:
                        pe.wait_ge(x_lo, KT * e + k + 1)
                    if n is not None and k == KT // 2:
                        root_rows(n)
                    for half in range(n_tok // w):
                        o, tok = PS[:, 2 * (b % 2) + half, 0:w], slice(half * w, (half + 1) * w)
                        nc.tensor.matmul(o, wp_h[:, b % 2, k], hi[:, k, tok], start=k == 0, stop=False)
                        nc.tensor.matmul(o, wp_h[:, b % 2, k], lo[:, k, tok], start=False, stop=False)
                        last = nc.tensor.matmul(o, wp_l[:, b % 2, k], hi[:, k, tok], start=False, stop=k == KT - 1)
                last.then_inc(blk_done, 1)

            ffn(0, 0, 0)

            pe.wait_ge(unit_free, 2 * FC)
            proj(0, 0, e=1, n=1)
            root_spread(1)
            proj(0, 1)
            pe.wait_ge(wdt_done, 1)
            for t in range(TC):
                for k in range(KT):
                    last = nc.tensor.matmul(PS[:, 7, 16 * t:16 * t + 16], X[:, k, t * P:(t + 1) * P], w_dtg[:, k], start=k == 0, stop=k == KT - 1)
            last.then_inc(dt_done, 1)
            with pe.Fori(1, B_V // 2) as i:
                proj(i, 0, free=(blk_free, 0))
                proj(i, 1, free=(blk_free, 0))
            pe.wait_ge(dt_out, 2)
            c7 = PS[:, 7, 0:P].rearrange("p (c h) -> p c h", c=TC)
            nc.tensor.matmul(c7[:, :, 0:8], trif, da[:, :, 0:8], start=True, stop=True)
            nc.tensor.matmul(c7[:, :, 8:16], trib, da[:, :, 8:16], start=True, stop=True)
            nc.tensor.matmul(PS[:, 6, 0:P], ones, da[:], start=True, stop=True).then_inc(cum_done, 1)
            with pe.Fori(B_V // 2, B_QK // 2) as i:
                proj(i, 0, free=(blk_free, 0))
                proj(i, 1, free=(blk_free, 0))

            for h in range(AH):
                pe.wait_ge(blk_free, B_V + h + 1)
                if h == 1:
                    pe.wait_ge(sp_step, 3)
                    pe.wait_ge(sp_act, 5)
                if h >= 2:
                    pe.wait_ge(v_back, h - 1)
                for k in range(KT):
                    last = nc.tensor.transpose(PS[:, 4 + 2 * (h % 2) + k // 4, k % 4 * P:(k % 4 + 1) * P], vo[:, h, k * P:(k + 1) * P], ident)
                last.then_inc(v_tr, 1)
            pe.wait_ge(v_back, AH)

            def swap(i, b):
                pe.wait_ge(blk_free, i * 2 + (b + 1))
                pe.wait_ge(qk_ready, i * 2 + (b - B_QK)) if (b - B_QK >= 2 or not isinstance(i, int)) else pe.wait_ge(dt_out, 1)
                for half in range(2):
                    last = nc.tensor.matmul(PS[:, 4 + 2 * (b % 2) + half], cst[:, ROPEP:ROPEP + P],
                                            X[:, one(i * 2 + (b - B_QK)), half * HALF:(half + 1) * HALF].rearrange("p o s -> p (o s)"), start=True, stop=True)
                last.then_inc(swap_done, 1)

            proj(0, B_QK, free=(blk_free, 0))
            proj(0, B_QK + 1, free=(blk_free, 0))
            swap(0, B_QK)
            with pe.Fori(0, 3) as i:
                proj(i, B_QK + 2, free=(blk_free, 0))
                swap(i, B_QK + 1)
                proj(i, B_QK + 3, free=(blk_free, 0))
                swap(i, B_QK + 2)
            swap(0, B_OUT - 1)

            def transposes(p, w):
                for k in range(4):
                    nc.tensor.transpose(PS[:, 4, k * P:(k + 1) * P], stage[:, p, k], ident)
                for g in range(2):
                    last = nc.tensor.transpose(PS[:, 5, g * P:(g + 1) * P], stage[:, p, 4 + g], ident)
                last.then_inc(w, 1)

            def states(p, w, bank=6):
                for g in range(2):
                    last = nc.tensor.matmul(PS[:, bank, 256 * g:256 * g + 256], b_n[:, p, g], xw[:, p, 4 * g:4 * g + 4].rearrange("p h d -> p (h d)"),
                                            start=True, stop=True)
                last.then_inc(w, 1)

            def decay_rows(p):
                for d in range(2):
                    for h in range(NH):
                        last = nc.tensor.matmul(PS[:, 2 * d + h // 4, h % 4 * P:(h % 4 + 1) * P],
                                                a_c[:, p, 8 * d + h:8 * d + h + 1].to_broadcast([P, P]), (trif, trib)[d], start=True, stop=True)
                last.then_inc(rows_done, 1)

            pe.wait_ge(first_a, 1)
            pe.wait_ge(blk_free, B_OUT)
            decay_rows(0)

            def turn_chunk(i, r):
                pe.wait_ge(stage_done, i * 2 + (r + 1))
                if r or not isinstance(i, int):
                    pe.wait_ge(nat_done, i * 2 + r)
                else:
                    pe.wait_ge(qk_ready, 8)
                transposes(r % 2, nat_tr)

            def add_chunk(i, r):
                pe.wait_ge(xw_done, i * 2 + (r + 2))
                pe.wait_ge(pb_done, i * 2 + max(r, 1))
                if r == 0:
                    pe.wait_ge(qk_ready, 9)
                states(r % 2, st_done, 6 + r % 2)

            turn_chunk(0, 0)
            with pe.Fori(0, 3) as i:
                for r in range(2):
                    turn_chunk(i, r + 1)
                    add_chunk(i, r)
            add_chunk(0, TC - 2)

            def front(i, c):
                p = c % 2
                pe.wait_ge(stage2, i * 2 + (c + 1))
                if c >= 1 or not isinstance(i, int):
                    pe.wait_ge(nat2_done, i * 2 + c)
                    pe.wait_ge(cb_used, i * 2 + c)
                transposes(p, nat2_tr)
                if c >= 1 or not isinstance(i, int):
                    pe.wait_ge(ecum_done, i * 2 + c)
                if c >= 1 or not isinstance(i, int):
                    decay_rows(p)
                pe.wait_ge(nat2_done, i * 2 + (c + 1))
                for g in range(2):
                    last = nc.tensor.matmul(PS[:, 5, 256 + g * P:256 + (g + 1) * P], stage[:, p, 4 + g], stage[:, p, 6 + g], start=True, stop=True)
                last.then_inc(cb_done, 1)

            def back(i, c, first=False):
                p = c % 2
                pe.wait_ge(xw2_done, i * 2 + (c + 1))
                if first:
                    pe.wait_ge(pb_done, TC)
                pe.wait_ge(carry_done, i * 2 + (c + 1))
                states(p, st2_done)
                pe.wait_ge(m_done, i * 2 + (c + 1))
                pe.wait_ge(xdt_done, i * 2 + (c + 2))
                pe.wait_ge(cdec_done, i * 2 + (c + 2))
                if not first:
                    pe.wait_ge(y_out, i * 2 + (c + 1))
                for h in range(NH):
                    r, col, hc = h % 2 * HD, h // 2 * P, slice(h * HD, (h + 1) * HD)
                    o = PS[r:r + HD, 7, col:col + P]
                    nc.tensor.matmul(o, xdt[:, p, 0, h], arg1[p][:, h], start=True, stop=False)
                    nc.tensor.matmul(o, xdt[:, p, 1, h], arg2[p][:, h], start=False, stop=False)
                    nc.tensor.matmul(o, carry[:, p, hc], ecum[p][:, 0, h], start=False, stop=False)
                    last = nc.tensor.matmul(o, pbc[:, p, hc], ecum[p][:, 1, h], start=False, stop=True)
                last.then_inc(y_done, 1)

            front(0, 0)
            with pe.Fori(0, TC // 2 - 1) as i:
                for c in range(2):
                    front(i, c + 1)
                    back(i, c)
            front(0, TC - 1)
            back(0, TC - 2)
            back(0, TC - 1)

            pe.wait_ge(ecum_done, TC)
            pe.wait_ge(zeros_done, 1)

            def scores(h, s):
                if s == 0:
                    pe.wait_ge(k_lo, h + 1)
                    pe.wait_ge(q_lo, h * 2 + 2)
                for t in range(2):
                    after(pe, exp_done, h, 16, 2 * s + t - 1)
                    qs = slice(s * P, (s + 1) * P)
                    for half in range(2):
                        o, kk = PS[:, 2 * t + half], slice(half * HALF, (half + 1) * HALF)
                        high = k_h[:, one(h), kk].rearrange("p o s -> p (o s)")
                        low = XR[:, one(h + AH), kk].rearrange("p o s -> p (o s)")
                        nc.tensor.matmul(o, q_h[:, t, qs], high, start=True, stop=False)
                        nc.tensor.matmul(o, q_h[:, t, qs], low, start=False, stop=False)
                        last = nc.tensor.matmul(o, q_l[:, t, qs], high, start=False, stop=True)
                    last.then_inc(sc_done, 1)

            def turn(h, s):
                pe.wait_ge(comb_done, h * TC + (s + 1))
                after(pe, at_lo, h, TC, s)
                for k in range(KT):
                    last = nc.tensor.matmul(PS[:, 4 + k // 4, k % 4 * P:(k % 4 + 1) * P], att[:, s % 2, k * P:(k + 1) * P],
                                            diag[:, s % 2], start=True, stop=True)
                last.then_inc(at_tr, 1)

            def values(h, j):
                if j == 0:
                    pe.wait_ge(v_lo, h + 1)
                pe.wait_ge(at_lo, h * TC + (2 * j + 2))
                after(pe, o_done, h, 4, max(j - 1, 0) + 1)
                o, qs = PS[:, 6 + j % 2, 0:2 * P], slice(j % 2 * 2 * P, (j % 2 + 1) * 2 * P)
                for k in range(KT):
                    nc.tensor.matmul(o, v_h[:, k], aT_h[:, k, qs], start=k == 0, stop=False)
                    nc.tensor.matmul(o, v_h[:, k], aT_l[:, k, qs], start=False, stop=False)
                    last = nc.tensor.matmul(o, v_l[:, k], aT_h[:, k, qs], start=False, stop=k == KT - 1)
                last.then_inc(pv_done, 1)

            def step(h, s, before=None, following=None, next_head=None):
                both = (before or (None, None), (h, s))
                for h_, s_ in both:
                    if h_ is not None and 2 <= s_ <= TC + 1:
                        turn(h_, s_ - 2)
                for h_, s_ in both:
                    if h_ is not None and s_ >= 4 and s_ % 2 == 0:
                        values(h_, s_ // 2 - 2)
                if following is not None:
                    scores(following, 0)
                elif h is not None and s < TC - 1:
                    scores(h, s + 1)

            scores(0, 0)
            body = heads_in_turn(step, lambda h: None)
            with pe.Fori(0, AH - 1) as h:
                body(h)
            body(AH - 1, last=True)

            pe.wait_ge(o_done, 4 * AH + 1)
            for g in range(6):
                if g < 2:
                    pe.wait_ge(gsum_done, g + 1)
                else:
                    pe.wait_ge(gsq_done, 3 + g)
                src, inv = (gsq[:, 2 * g], INV256) if g < 2 else (gsq[:, 2 + g], INV128)
                for t in range(TC):
                    last = nc.tensor.matmul(PS[:, 6, 8 * g + t:8 * g + t + 1], src[:, t * P:(t + 1) * P], cst[:, inv:inv + 1], start=True, stop=True)
            last.then_inc(grow_done, 1)
            pe.wait_ge(groot_done, 1)
            for g in range(6):
                if g >= 2:
                    pe.wait_ge(gs_free, (2, 4, 5, 6)[g - 2])
                for t in range(TC):
                    last = nc.tensor.matmul(PS[:, 2 * (g % 2) + t // 4, t % 4 * P:(t % 4 + 1) * P],
                                            rg[:, 2, 8 * g + t:8 * g + t + 1].to_broadcast([P, P]), ident, start=True, stop=True)
                last.then_inc(gs_done, 1)
            pe.wait_ge(gs_free, KT)

            proj(0, B_OUT, e=2)
            pe.wait_ge(msum_done, 1)
            for t in range(2):
                last = nc.tensor.matmul(PS[:, 6, t:t + 1], qx[:, 4, t * P:(t + 1) * P], cst[:, INV1024:INV1024 + 1], start=True, stop=True)
            last.then_inc(mrow_done, 1)
            proj(0, B_OUT + 1)
            out2 = (x_done, XB[2] - KT - B_OUT)
            with pe.Fori(1, 4) as i:
                proj(i, B_OUT, free=out2)
                proj(i, B_OUT + 1, free=out2)
            pe.wait_ge(mroot_done, 1)
            for t in range(2):
                last = nc.tensor.matmul(PS[:, 7, t * P:(t + 1) * P], rm[:, 2, t:t + 1].to_broadcast([P, P]), ident, start=True, stop=True)
            last.then_inc(mspread_done, 1)
            pe.wait_ge(mem_lo, 1)
            proj(0, B_KV, mem_h, mem_l, M, free=out2)
            root_rows(2)
            proj(0, B_KV + 1, mem_h, mem_l, M, free=out2)
            root_spread(2)
            out3 = (blk_free, -KT)
            with pe.Fori(1, 8) as i:
                proj(i, B_KV, mem_h, mem_l, M, free=out3)
                proj(i, B_KV + 1, mem_h, mem_l, M, free=out3)
            pe.wait_ge(blk_free, B_Q - KT)
            pe.wait_ge(r_ready, 3)
            pe.wait_ge(mr_done, 1)
            for h in range(AH):
                for m in range(2):
                    for e in range(2):
                        last = nc.tensor.transpose(PS[:, 4 + h, m * M + e * P:m * M + (e + 1) * P], kv[:, 8 + 2 * h + e, m * P:(m + 1) * P], ident)
                if h % 2:
                    last.then_inc(cv_tr, 1)
            pe.wait_ge(x_lo, 4 * KT)
            with pe.Fori(0, 4) as i:
                proj(i, B_Q, free=out3)
                proj(i, B_Q + 1, free=out3)

            pe.wait_ge(ck_lo, 1)
            pe.wait_ge(cv_back, 2)

            def scores(i, j):
                pe.wait_ge(cq_lo, i * 2 + (j + 1))
                h, p = i + j // 2, j % 2
                after(pe, cexp_done, i, 2, j - 1)
                for t in range(4):
                    o, qs = PS[:, 2 * p + t // 2, t % 2 * M:(t % 2 + 1) * M], slice(t * P, (t + 1) * P)
                    for k in range(2):
                        high, low = (c[:, one(h * 2 + k)].rearrange("p o m -> p (o m)") for c in (ck_h, ck_l))
                        nc.tensor.matmul(o, cq_h[:, p, k, qs], high, start=k == 0, stop=False)
                        nc.tensor.matmul(o, cq_h[:, p, k, qs], low, start=False, stop=False)
                        last = nc.tensor.matmul(o, cq_l[:, p, k, qs], high, start=False, stop=k == 1)
                last.then_inc(cs_done, 1)

            def turn(i, j):
                pe.wait_ge(cnorm_done, i * 2 + (j + 1))
                after(pe, cp_lo, i, 2, j)
                for t in range(4):
                    for m in range(2):
                        last = nc.tensor.transpose(PS[:, 4 + m, t * P:(t + 1) * P], cp[:, j % 2, t, m * P:(m + 1) * P], ident)
                last.then_inc(cp_tr, 1)

            def values(i, j):
                pe.wait_ge(cp_lo, i * 2 + (j + 1))
                if j % 2 == 0:
                    pe.wait_ge(cv_lo, i + (j // 2 + 1))
                after(pe, co_done, i, 2, j + 1)
                for e in range(2):
                    for m in range(2):
                        ev = slice(e * P, (e + 1) * P)
                        o = PS[:, 6 + e]
                        nc.tensor.matmul(o, cv_h[:, m, ev], cpT_h[:, j % 2, m], start=m == 0, stop=False)
                        nc.tensor.matmul(o, cv_h[:, m, ev], cpT_l[:, j % 2, m], start=False, stop=False)
                        last = nc.tensor.matmul(o, cv_l[:, m, ev], cpT_h[:, j % 2, m], start=False, stop=m == 1)
                last.then_inc(cpv_done, 1)

            def step(i, j):
                if in_groups(i, j - 1):
                    turn(i, j - 1)
                if in_groups(i, j - 2):
                    values(i, j - 2)
                if in_groups(i, j + 1):
                    scores(i, j + 1)

            scores(0, 0)
            groups(pe, step)

            pe.wait_ge(co_done, 2 * AH + 1)
            proj(0, B_O, e=4)
            proj(0, B_O + 1)
            out4 = (x_done, XB[3] - KT - B_O)
            with pe.Fori(1, 4) as i:
                proj(i, B_O, free=out4)
                proj(i, B_O + 1, free=out4)
            pe.wait_ge(x_done, XB[3])
            ffn(1, 3, 5)
            root_rows(4)
            root_spread(4)

        @block.vector
        def _(dve):
            own = Steps(dve, dve_own)
            unused = rn[:, 2, TC:16]
            for j, w in enumerate((conv_done, conv_silu, qk_ready, xw_done, st_done, xdt_done, cdec_done, cb_done,
                                   y_done, y_out, st2_done, carry_done, pv_done, o_done, cpv_done, co_done)):
                dve.memset(unused[64 * (j // 8):64 * (j // 8) + 64, j % 8:j % 8 + 1], 0.0).then_inc(w, 1)

            def low_x(e, k, src=None):
                dve.wait_ge(x_hi, KT * e + k + 1)
                nc.vector.tensor_tensor(XL[:, k], X[:, k] if src is None else src, XH[:, k].bitcast(F32), ALU.subtract).then_inc(x_lo, 1)

            def root(n):
                dve.wait_ge(rs_done, n + 1)
                own.done(nc.vector.tensor_scalar(rn[:, 0, 0:TC], PS[:, 6, 0:TC], EPS, None, ALU.add))
                nc.vector.reciprocal(rn[:, 1, 0:TC], rn[:, 0, 0:TC]).then_inc(rs_inv, 1)
                dve.wait_ge(rb_done, n + 1)
                nc.vector.tensor_copy(RB[:], PS[:, 4:6].rearrange("p a b -> p (a b)")).then_inc(r_ready, 1)
                dve.wait_ge(r_ready, n + 1)

            def ffn(f, n, gain, before, after):
                c0, u0 = f * FC, 2 * f * FC

                def split_gu(i, c, pieces=range(4)):
                    for q in pieces:
                        dve.wait_ge(gu_hi, i * 8 + (4 * (c0 + c) + q + 1))
                        for k in range(2 * q, 2 * q + 2):
                            last = nc.vector.scalar_tensor_tensor(
                                out=wgu_l[:, k], in0=wgu_raw[:, c % 2, k], scalar=par[:, gain + k:gain + k + 1],
                                in1=wgu_h[:, k].bitcast(F32), op0=ALU.mult, op1=ALU.subtract)
                        last.then_inc(gu_lo, 1)

                def split_wd(i, c):
                    dve.wait_ge(wd_hi, i * 2 + (c0 + c + 1))
                    nc.vector.tensor_tensor(wd_l[:, c], wd_raw[:, c], wd_h[:, c].bitcast(F32),
                                            ALU.subtract).then_inc(wd_lo, 1)

                def unit(i, u):
                    b, tok = 2 * (u % 2), slice(u % 2 * HALF, (u % 2 + 1) * HALF)
                    dve.wait_ge(unit_done, i * 4 + (u0 + u + 1))
                    nc.vector.tensor_tensor(tg[:, u % 2], PS[:, b], RB[:, tok], ALU.mult).then_inc(tg_done, 1)
                    nc.vector.tensor_tensor(tu[:, u % 2], PS[:, b + 1], RB[:, tok], ALU.mult).then_inc(unit_free, 1)
                    dve.wait_ge(silu_done, i * 4 + (u0 + u + 1))
                    dve.wait_ge(unit_free, i * 4 + (u0 + u + 1))
                    nc.vector.tensor_tensor(ta[:, u % 2], tsl[:, u % 2], tu[:, u % 2], ALU.mult).then_inc(ta_done, 1)
                    dve.wait_ge(hid_hi, i * 4 + (u0 + u + 1))
                    nc.vector.tensor_tensor(hid_l[:, u // 2, tok], ta[:, u % 2], hid_h[:, u // 2, tok].bitcast(F32),
                                            ALU.subtract).then_inc(hid_lo, 1)

                def add_down(i, m):
                    dve.wait_ge(down_done, i * KT + (KT * PAIRS * f + m + 1))
                    b = 4 + 2 * (m % 2)
                    nc.vector.scalar_tensor_tensor(out=X[:, m], in0=PS[:, b:b + 2].rearrange("p a b -> p (a b)"), scalar=0.5, in1=X[:, m],
                                                   op0=ALU.mult, op1=ALU.add).then_inc(x_done, 1)

                split_gu(0, 0, range(2 * f, 4))
                before()
                root(n)

                def pair(i, last=False):
                    unit(i, 0)
                    split_wd(i, 0)
                    split_wd(i, 1)
                    split_gu(i, 1)
                    unit(i, 1)
                    unit(i, 2)
                    if not last:
                        split_gu(i, 2, range(3))
                    unit(i, 3)
                    if not last:
                        split_gu(i, 2, range(3, 4))
                        for m in range(KT):
                            add_down(i, m)

                pair(0)
                with dve.Fori(1, PAIRS - 1) as i:
                    pair(i)
                pair(PAIRS - 1, last=True)
                after(add_down)

            def low_gu_first():
                for q in range(2):
                    dve.wait_ge(gu_hi, 4 * FC + q + 1)
                    for k in range(2 * q, 2 * q + 2):
                        last = dve.scalar_tensor_tensor(out=wgu_l[:, k], in0=wgu_raw[:, 0, k], scalar=par[:, G_FFN2 + k:G_FFN2 + k + 1],
                                                        in1=wgu_h[:, k].bitcast(F32), op0=ALU.mult, op1=ALU.subtract)
                    last.then_inc(gu_lo, 1)

            def split_weights(i, b, gain, src):
                for k in range(KT):
                    if k % 4 == 0:
                        dve.wait_ge(wp_hi, i * 4 + (2 * b + k // 4 + 1))
                    last = nc.vector.scalar_tensor_tensor(
                        out=wp_l[:, b % 2, k], in0=wp_raw[:, b % 2, k], scalar=src[:, gain + k:gain + k + 1],
                        in1=wp_h[:, b % 2, k].bitcast(F32), op0=ALU.mult, op1=ALU.subtract)
                last.then_inc(wp_lo, 1)

            def banks(b):
                return PS[:, 2 * (b % 2):2 * (b % 2) + 2].rearrange("p a b -> p (a b)")

            def to_mixer(add_down):
                split_weights(0, 0, G_MIX, par)
                for m in range(KT):
                    add_down(PAIRS - 1, m)
                    if m:
                        low_x(1, m - 1)
                low_x(1, KT - 1)
                dve.wait_ge(s_wdt, 16)
                nc.vector.tensor_tensor(w_dtg[:], dt_raw[:], par[:, G_MIX:G_MIX + KT].unsqueeze(2).to_broadcast([P, KT, 16]),
                                        ALU.mult).then_inc(wdt_done, 1)
                root(1)

            def x_loaded():
                for k in range(KT):
                    low_x(0, k)
                for k in range(KT):
                    dve.wait_ge(sq_done, k + 1)
                    if k == 0:
                        last = dve.tensor_copy(ssum[:], sq[:, 0])
                    else:
                        last = dve.tensor_tensor(ssum[:], ssum[:], sq[:, k % 2], ALU.add)
                    last.then_inc(sq_added, 1)
                    dve.wait_ge(sq_added, k + 1)

            dve.wait_ge(s_par, 16)
            ffn(0, 0, G_FFN1, x_loaded, to_mixer)

            dve.memset(craw[:, 0:2], 0.0)
            own.done(dve.memset(craw[:, S + 2:S + 4], 0.0))

            def conv_block(i, j):
                dve.wait_ge(blk_done, i * 2 + j + 1)
                dve.wait_ge(conv_done, i * 2 + (j + 1))
                nc.vector.tensor_tensor(craw[:, 2:S + 2], banks(j), RB[:], ALU.mult).then_inc(blk_free, 1)
                dve.wait_ge(blk_free, i * 2 + j + 1)
                dve.wait_ge(conv_silu, i * 2 + 1)
                a = conv_acc[:, j]
                own.done(nc.vector.tensor_scalar(a, craw[:, 0:S], par[:, one(i * 10 + (CONVW + 5 * j))], None, ALU.mult))
                for t in range(1, 5):
                    ins = nc.vector.scalar_tensor_tensor(out=a, in0=craw[:, t:t + S], scalar=par[:, one(i * 10 + (CONVW + 5 * j + t))],
                                                         in1=a, op0=ALU.mult, op1=ALU.add)
                    if t < 4:
                        own.done(ins)
                    else:
                        ins.then_inc(conv_done, 1)

            base = own.n
            with dve.Fori(0, (B_Z - B_XBC) // 2) as i:
                for j in range(2):
                    own.n = i * 8 + (base + 4 * j)
                    split_weights(i, j + 1, G_MIX, par)
                    conv_block(i, j)
            own.n = base + 4 * 8
            dve.wait_ge(dt_done, 1)
            own.done(nc.vector.tensor_tensor(dt_raw[:], PS[:, 7, 0:P].rearrange("p (c h) -> p c h", c=TC),
                                             rn[:, 2, 0:TC].unsqueeze(2).to_broadcast([P, TC, 16]), ALU.mult))
            dve.tensor_tensor(dt_raw[:], dt_raw[:], par[:, DTBIAS:DTBIAS + 16].unsqueeze(1).to_broadcast([P, TC, 16]),
                              ALU.add).then_inc(dt_out, 1)
            split_weights(0, B_Z + 1, G_MIX, par)
            t1, t2, ex = etot, cum, w_state
            dve.wait_ge(dt_out, 1)
            own.done(dve.tensor_scalar(t1[:], dt_raw[:], -1.0, None, ALU.mult))
            nc.vector.tensor_tensor(t1[:], t1[:], dt_raw[:], ALU.max).then_inc(sp_step, 1)
            dve.wait_ge(sp_act, 1)
            dve.tensor_scalar(t1[:], ex[:], 1.0, None, ALU.add).then_inc(sp_step, 1)
            dve.wait_ge(sp_step, 2)
            own.done(nc.vector.tensor_scalar(dt_tmp[:], t1[:], 1.0, None, ALU.subtract))
            own.done(nc.vector.tensor_scalar(dt[:], dt_tmp[:], 0.0, None, ALU.is_equal))
            own.done(nc.vector.tensor_tensor(dt_tmp[:], dt_tmp[:], dt[:], ALU.add))
            dve.wait_ge(sp_act, 2)
            own.done(nc.vector.tensor_tensor(t2[:], t2[:], dt[:], ALU.add))
            own.done(nc.vector.reciprocal(dt_tmp[:], dt_tmp[:]))
            own.done(nc.vector.tensor_tensor(t2[:], t2[:], dt_tmp[:], ALU.mult))
            own.done(nc.vector.tensor_tensor(t2[:], t2[:], ex[:], ALU.mult))
            own.done(nc.vector.tensor_scalar(dt_raw[:], dt_raw[:], 0.0, None, ALU.max))
            own.done(nc.vector.tensor_tensor(dt[:], dt_raw[:], t2[:], ALU.add))
            dve.wait_ge(sp_act, 3)
            own.done(nc.vector.tensor_scalar(rn[:, 1, :], rn[:, 0, :], -1.0, None, ALU.mult))
            dve.tensor_tensor(da[:], dt[:], rn[:, 1, :].unsqueeze(1).to_broadcast([P, TC, 16]), ALU.mult).then_inc(dt_out, 1)
            with dve.Fori(0, (B_V - B_Z) // 2) as i:
                for j in range(2):
                    dve.wait_ge(blk_done, i * 2 + (B_Z + j + 1))
                    dve.wait_ge(conv_silu, i * 2 + (B_Z + j))
                    nc.vector.tensor_tensor(conv_acc[:, j], banks(j), RB[:], ALU.mult).then_inc(blk_free, 1)
                    split_weights(i, B_Z + j + 2, G_MIX, par)
            dve.wait_ge(cum_done, 1)
            own.done(dve.tensor_copy(cum[:], PS[:, 7, 0:P].rearrange("p (c h) -> p c h", c=TC)))
            dve.tensor_tensor(dt_tmp[:], PS[:, 6, 0:P].rearrange("p (c h) -> p c h", c=TC), cum[:], ALU.subtract).then_inc(sp_step, 1)
            dve.wait_ge(sp_act, 4)
            dve.tensor_tensor(w_state[:], w_state[:], dt[:], ALU.mult).then_inc(sp_step, 1)
            with dve.Fori(0, (B_QK - B_V) // 2) as i:
                for j in range(2):
                    dve.wait_ge(blk_done, i * 2 + (B_V + j + 1))
                    nc.vector.tensor_tensor(vo[:, one(i * 2 + j)].rearrange("p o s -> p (o s)"), banks(j), RB[:], ALU.mult).then_inc(blk_free, 1)
                    split_weights(i, B_V + j + 2, G_MIX, par)

            def turn_qk(i, j, nstep):
                xq = X[:, one(i * 2 + j)].rearrange("p o s -> p (o s)")
                t = craw[:, 0:S]
                dve.wait_ge(swap_done, i * 2 + (j + 1))
                own.n = nstep
                dve.wait_ge(qk_ready, i * 2 + (j + 1))
                own.mark(nc.vector.tensor_tensor(t, PS[:, 4 + 2 * (j % 2):6 + 2 * (j % 2)].rearrange("p a b -> p (a b)"), rope[:, 1], ALU.mult))
                own.done(nc.vector.tensor_tensor(xq, xq, rope[:, 0], ALU.mult))
                nc.vector.tensor_tensor(xq, xq, t, ALU.add).then_inc(qk_ready, 1)

            def out_qk(i, j):
                dve.wait_ge(blk_done, i * 2 + (B_QK + j + 1))
                nc.vector.tensor_tensor(X[:, one(i * 2 + j)].rearrange("p o s -> p (o s)"), banks(j), RB[:], ALU.mult).then_inc(blk_free, 1)

            for h in range(AH):
                dve.wait_ge(v_tr, h + 1)
                b = 4 + 2 * (h % 2)
                dve.tensor_copy(vo[:, h], PS[:, b:b + 2].rearrange("p a b -> p (a b)")).then_inc(v_back, 1)
            dve.wait_ge(s_spill, 16)
            dve.wait_ge(s_rope, 16)
            out_qk(0, 0)
            base = own.n
            with dve.Fori(0, 3) as i:
                for j in range(2):
                    split_weights(i, B_QK + j + 2, G_MIX, par)
                    out_qk(i, j + 1)
                    turn_qk(i, j, i * 4 + (base + 2 * j))
            out_qk(0, 7)
            turn_qk(0, 6, base + 12)
            turn_qk(0, 7, base + 14)

            dve.wait_ge(blk_done, B_OUT)
            nc.vector.memset(carry[:, 0], 0.0)
            dve.memset(prev_b[:, TC - 1], 0.0).then_inc(pb_done, 1)

            def per_head(t, c, d, n):
                return t[:, one(c), 8 * d:8 * d + 8].rearrange("p o h -> p (o h)").unsqueeze(2).to_broadcast([P, NH, n])

            def heads(ap):
                return ap.rearrange("p (h d) -> p h d", h=NH)

            def carry_back(i, r):
                c = (TC - 1 - r) if isinstance(i, int) else i * -2 + (TC - 1 - r)
                dve.wait_ge(pb_done, i * 2 + (r + 1))
                dst = prev_b[:, one(c - 1)].rearrange("p o (h d) -> p (o h) d", h=NH)
                dve.tensor_tensor(dst, prev_b[:, one(c)].rearrange("p o (h d) -> p (o h) d", h=NH), per_head(etot, c, 1, HD), ALU.mult).then_inc(pb_mul, 1)
                dve.wait_ge(pb_mul, i * 2 + (r + 1))
                dve.wait_ge(st_done, i * 2 + (r + 2))
                dve.tensor_tensor(dst, dst, heads(PS[:, 6 + r % 2]), ALU.add).then_inc(pb_done, 1)

            def first_part(i, c, nstep):
                own.n = nstep
                dve.wait_ge(rows_done, i * 2 + (c + 1))
                cc = i * 2 + c
                after(dve, y_done, i, 2, c)
                a1, a2 = arg1[c % 2], arg2[c % 2]
                for d, a in enumerate((a1, a2)):
                    own.mark(dve.tensor_tensor(a[:], PS[:, 2 * d:2 * d + 2].rearrange("p a (h l) -> p (a h) l", l=P), per_head(cum, cc, d, P), ALU.subtract))
                own.wait()
                own.done(dve.tensor_scalar(a2[:], a2[:], 0.0, None, ALU.min))
                dve.scalar_tensor_tensor(out=a1[:].rearrange("p h l -> p (h l)"), in0=a1[:].rearrange("p h l -> p (h l)"), scalar=0.0,
                                         in1=a2[:].rearrange("p h l -> p (h l)"), op0=ALU.min, op1=ALU.add).then_inc(arg_done, 1)

            def masked(i, c):
                dve.wait_ge(cb_done, i * 2 + (c + 2))
                src = PS[:, 5, 256:512].rearrange("p (g l) -> p g l", g=2)
                dve.tensor_tensor(cb[:, 0], src, trif.unsqueeze(1).to_broadcast([P, 2, P]), ALU.mult)
                dve.tensor_tensor(cb[:, 1], src, trib.unsqueeze(1).to_broadcast([P, 2, P]), ALU.mult).then_inc(cb_used, 1)
                dve.wait_ge(cb_used, i * 2 + (c + 1))

            def second_part(i, c):
                dve.wait_ge(e_done, i * 2 + (c + 1))
                e4 = arg1[c % 2][:].rearrange("p (g r) l -> p g r l", g=2)
                m4 = arg2[c % 2][:].rearrange("p (g r) l -> p g r l", g=2)
                own.done(dve.tensor_tensor(m4, e4, cb[:, 1].unsqueeze(2).to_broadcast([P, 2, 4, P]), ALU.mult))
                dve.tensor_tensor(e4, e4, cb[:, 0].unsqueeze(2).to_broadcast([P, 2, 4, P]), ALU.mult).then_inc(m_done, 1)

            def third_part(i, c, nstep):
                p, cc = c % 2, i * 2 + c
                own.n = nstep
                dve.wait_ge(y_done, i * 2 + (c + 2))
                for k in range(4):
                    ins = dve.scalar_tensor_tensor(out=tmps[:, k], in0=xbc[:, k, chunk(cc)], scalar=par[:, DSKIP + k:DSKIP + k + 1],
                                                   in1=PS[:, 7, k * P:(k + 1) * P], op0=ALU.mult, op1=ALU.add)
                own.done(ins)
                dve.tensor_tensor(zy[:, :, chunk(cc)], zy[:, :, chunk(cc)], tmps[:], ALU.mult).then_inc(y_out, 1)
                dve.wait_ge(st2_done, i * 2 + (c + 2))
                own.done(dve.tensor_tensor(heads(carry[:, 1 - p]), heads(carry[:, p]), per_head(etot, cc, 0, HD), ALU.mult))
                dve.tensor_tensor(carry[:, 1 - p], carry[:, 1 - p], PS[:, 6], ALU.add).then_inc(carry_done, 1)
                dve.wait_ge(carry_done, i * 2 + (c + 2))

            def split_q(h):
                for t in range(2):
                    r = slice(t * HD, (t + 1) * HD)
                    dve.wait_ge(q_hi, h * 2 + (t + 1))
                    dve.tensor_tensor(q_l[r, t], X[r, one(h)].rearrange("p o s -> p (o s)"), q_h[r, t].bitcast(F32), ALU.subtract).then_inc(q_lo, 1)

            def split_k(h):
                dve.wait_ge(k_hi, h + 1)
                k = X[:, one(h + AH)]
                dve.tensor_tensor(XR[:, one(h + AH)], k, k_h[:, one(h)].bitcast(F32), ALU.subtract).then_inc(k_lo, 1)

            base = own.n
            first_part(0, 0, base)
            with dve.Fori(0, 3) as i:
                for r in range(2):
                    carry_back(i, r)
            carry_back(0, 6)
            masked(0, 0)
            second_part(0, 0)
            with dve.Fori(0, TC // 2 - 1) as i:
                for c in range(2):
                    first_part(i, c + 1, i * 12 + (base + 6 * c + 4))
                    masked(i, c + 1)
                    second_part(i, c + 1)
                    third_part(i, c, i * 12 + (base + 6 * c + 8))
            first_part(0, TC - 1, base + 6 * TC - 8)
            masked(0, TC - 1)
            second_part(0, TC - 1)
            third_part(0, TC - 2, base + 6 * TC - 4)
            split_k(0)
            split_q(0)
            third_part(0, TC - 1, base + 6 * TC - 2)
            own.n = base + 6 * TC

            dve.wait_ge(y_out, TC + 1)
            lv = par[:, LAM:LAM + 4 * HD].rearrange("p (a b d) -> p a b d", a=2, b=2)
            own.done(dve.tensor_tensor(lam_t[:], lv[:, :, 0], lv[:, :, 1], ALU.mult))
            dve.tensor_reduce(lam[:, 0:2], lam_t[:], AX.X, ALU.add).then_inc(lam_sum, 1)
            dve.wait_ge(lam_exp, 1)
            own.done(dve.tensor_tensor(lam[:, 4:5], lam[:, 3:4], lam[:, 2:3], ALU.subtract))
            own.done(dve.tensor_scalar(lam[:, 5:6], lam[:, 4:5], LAMBDA_INIT, None, ALU.subtract))
            dve.tensor_copy(g_out[:, 0:4], par[:, G_SSD:G_SSD + 4])
            dve.memset(g_out[:, 8:16], 1.0)
            dve.tensor_scalar(g_out[:, 4:8], par[:, G_SUB:G_SUB + 1].to_broadcast([P, 4]), 1.0 - LAMBDA_INIT, None, ALU.mult).then_inc(g_done, 1)

            def split_v(h):
                dve.wait_ge(v_hi, h + 1)
                dve.tensor_tensor(v_l[:], vo[:, one(h)].rearrange("p o (k e) -> p (o k) e", e=P), v_h[:].bitcast(F32), ALU.subtract).then_inc(v_lo, 1)

            def largest(h, s):
                for t in range(2):
                    dve.wait_ge(sc_done, h * 16 + (2 * s + t + 1))
                    dve.tensor_reduce(stat[:, s % 2, t, 0:1], PS[:, 2 * t:2 * t + 2].rearrange("p a b -> p (a b)"), AX.X, ALU.max).then_inc(max_done, 1)
                    dve.wait_ge(max_done, h * 16 + (2 * s + t + 1))
                    dve.tensor_scalar(stat[:, s % 2, 2 + t, 0:1], stat[:, s % 2, t, 0:1], -0.125, None, ALU.mult).then_inc(nm_done, 1)

            def ratio(h, s):
                z = stat[:, s % 2]
                dve.wait_ge(exp_done, h * 16 + (2 * s + 2))
                after(dve, comb_done, h, TC, s - 1)
                dve.reciprocal(z[:, 6:8, 0:1], z[:, 4:6, 0:1]).then_inc(inv_done, 1)
                dve.wait_ge(inv_done, h * TC + (s + 1))
                dve.tensor_scalar(z[:, 7, 1:2], z[:, 7, 0:1], z[:, 4, 0:1], lam[:, 5:6], ALU.mult, ALU.mult).then_inc(ratio_done, 1)

            def low(h, s):
                dve.wait_ge(at_hi, h * TC + (s + 1))
                sl = slice(s % 4 * P, (s % 4 + 1) * P)
                dve.tensor_tensor(aT_l[:, :, sl], PS[:, 4:6].rearrange("p a (k q) -> p (a k) q", q=P), aT_h[:, :, sl].bitcast(F32),
                                  ALU.subtract).then_inc(at_lo, 1)

            def values(h, j):
                dve.wait_ge(pv_done, h * 4 + (j + 2))
                dve.tensor_scalar(vo[:, one(h), j * 2 * P:(j + 1) * 2 * P].rearrange("p o s -> p (o s)"), PS[:, 6 + j % 2, 0:2 * P],
                                  1.0, None, ALU.mult).then_inc(o_done, 1)

            def step(h, s, before=None, following=None, next_head=None):
                both = (before or (None, None), (h, s))
                if h is not None:
                    largest(h, s)
                if s == TC - 3 and next_head is not None:
                    split_k(next_head)
                if following is not None:
                    split_q(following)
                for h_, s_ in both:
                    if h_ is not None and 2 <= s_ <= TC + 1:
                        low(h_, s_ - 2)
                if h is not None:
                    ratio(h, s)
                for h_, s_ in both:
                    if h_ is not None and s_ >= 5 and s_ % 2 == 1:
                        values(h_, (s_ - 5) // 2)
                    if h_ is not None and s_ == TC + 2:
                        values(h_, 3)

            body = heads_in_turn(step, split_v)
            with dve.Fori(0, AH - 1) as h:
                body(h)
            body(AH - 1, last=True)

            dve.wait_ge(grow_done, 1)
            own.done(dve.tensor_scalar(rg[:, 0], PS[:, 6, 0:48], EPS, None, ALU.add))
            dve.reciprocal(rg[:, 1], rg[:, 0]).then_inc(ginv_done, 1)
            split_weights(0, B_OUT, 0, g_out)
            for g in range(6):
                dve.wait_ge(gs_done, g + 1)
                r = PS[:, 2 * (g % 2):2 * (g % 2) + 2].rearrange("p a b -> p (a b)")
                tiles_ = [zy[:, 2 * g], zy[:, 2 * g + 1]] if g < 2 else [vo[:, g - 2]]
                k0 = 2 * g if g < 2 else 2 + g
                for n_, y in enumerate(tiles_):
                    dve.tensor_tensor(y, y, r, ALU.mult).then_inc(gs_free, 1)
                for n_, y in enumerate(tiles_):
                    low_x(2, k0 + n_, y)
            dve.wait_ge(mem_hi, 1)
            dve.tensor_tensor(mem_l[:], memX[:], mem_h[:].bitcast(F32), ALU.subtract).then_inc(mem_lo, 1)
            dve.wait_ge(mrow_done, 1)
            own.done(dve.tensor_scalar(rm[:, 0], PS[:, 6, 0:2], EPS, None, ALU.add))
            dve.reciprocal(rm[:, 1], rm[:, 0]).then_inc(minv_done, 1)

            def residual(n, b0, b1, gain, src, following):
                def add(i, j):
                    dve.wait_ge(blk_done, i * 2 + (b0 + j + 1))
                    x = X[:, one(i * 2 + j)].rearrange("p o s -> p (o s)")
                    dve.tensor_tensor(x, banks(j), x, ALU.add).then_inc(x_done, 1)
                with dve.Fori(0, (b1 - b0) // 2 - 1) as i:
                    for j in range(2):
                        split_weights(i, b0 + j + 1, gain, src)
                        add(i, j)
                split_weights(0, b1 - 1, gain, src)
                add(KT // 2 - 1, 0)
                following()
                add(KT // 2 - 1, 1)

            for q in range(4):
                dve.wait_ge(s_back[q], 16)
            residual(2, B_OUT, B_KV, 0, g_out, lambda: split_weights(0, B_KV, G_MEM, par))
            dve.wait_ge(mspread_done, 1)
            dve.tensor_copy(RM[:], PS[:, 7, 0:M]).then_inc(mr_done, 1)
            dve.wait_ge(mr_done, 1)
            split_weights(0, B_KV + 1, G_MEM, par)
            dve.wait_ge(rs_done, 3)
            own.done(nc.vector.tensor_scalar(rn[:, 0, 0:TC], PS[:, 6, 0:TC], EPS, None, ALU.add))
            nc.vector.reciprocal(rn[:, 1, 0:TC], rn[:, 0, 0:TC]).then_inc(rs_inv, 1)

            def kv_out(i, j):
                dve.wait_ge(blk_done, i * 2 + (B_KV + j + 1))
                dve.tensor_tensor(kv[:, one(i * 2 + j)].rearrange("p o m -> p (o m)"), PS[:, 2 * j, 0:M], RM[:], ALU.mult).then_inc(blk_free, 1)

            kv_out(0, 0)
            with dve.Fori(0, (B_Q - B_KV) // 2 - 1) as i:
                split_weights(i, B_KV + 2, G_MEM, par)
                kv_out(i, 1)
                split_weights(i, B_KV + 3, G_MEM, par)
                dve.wait_ge(blk_done, i * 2 + (B_KV + 3))
                dve.tensor_tensor(kv[:, one(i * 2 + 2)].rearrange("p o m -> p (o m)"), PS[:, 0, 0:M], RM[:], ALU.mult).then_inc(blk_free, 1)
                dve.wait_ge(x_hi, i + (3 * KT + 1))
                dve.tensor_tensor(XL[:, one(i)], X[:, one(i)], XH[:, one(i)].bitcast(F32), ALU.subtract).then_inc(x_lo, 1)
            low_x(3, KT - 1)
            split_weights(0, B_Q, G_XQ, par)
            kv_out(7, 1)
            dve.wait_ge(rb_done, 3)
            dve.tensor_copy(RB[:], PS[:, 4:6].rearrange("p a b -> p (a b)")).then_inc(r_ready, 1)
            dve.wait_ge(r_ready, 3)
            dve.wait_ge(cv_tr, 2)
            dve.tensor_copy(kv[:, 12:16], PS[:, 6:8].rearrange("p h (m e) -> p (h m) e", m=2)).then_inc(cv_back, 1)
            dve.wait_ge(ck_hi, 1)
            dve.tensor_tensor(ck_l[:], kv[:, 0:8], ck_h[:].bitcast(F32), ALU.subtract).then_inc(ck_lo, 1)

            def q_out(i, j):
                dve.wait_ge(blk_done, i * 2 + (B_Q + j + 1))
                dve.tensor_tensor(qx[:, one(i * 2 + j)].rearrange("p o s -> p (o s)"), banks(j), RB[:], ALU.mult).then_inc(blk_free, 1)
            with dve.Fori(0, (B_O - B_Q) // 2 - 1) as i:
                for j in range(2):
                    split_weights(i, B_Q + j + 1, G_XQ, par)
                    q_out(i, j)
            split_weights(0, B_O - 1, G_XQ, par)
            q_out(3, 0)
            q_out(3, 1)

            dve.wait_ge(cv_back, 2)

            def split_q(i, j):
                h, p = i + j // 2, j % 2
                dve.wait_ge(cq_hi, i * 2 + (j + 1))
                dve.tensor_tensor(cq_l[:, p], qx[:, bass.ds(h * 2, 2), p * HALF:(p + 1) * HALF], cq_h[:, p].bitcast(F32), ALU.subtract).then_inc(cq_lo, 1)

            def split_v(i, j):
                dve.wait_ge(cv_hi, i + (j // 2 + 1))
                dve.tensor_tensor(cv_l[:], kv[:, bass.ds((i + j // 2) * 2 + 8, 2)], cv_h[:].bitcast(F32), ALU.subtract).then_inc(cv_lo, 1)

            def largest(i, j):
                p = j % 2
                dve.wait_ge(cs_done, i * 2 + (j + 1))
                dve.tensor_reduce(cstat[:, p, 0], PS[:, 2 * p:2 * p + 2].rearrange("p a (t m) -> p (a t) m", t=2), AX.X, ALU.max).then_inc(cmax_done, 1)
                dve.wait_ge(cmax_done, i * 2 + (j + 1))
                dve.tensor_scalar(cstat[:, p, 1], cstat[:, p, 0], -0.0625, None, ALU.mult).then_inc(cnm_done, 1)

            def normalise(i, j):
                p = j % 2
                dve.wait_ge(cexp_done, i * 2 + (j + 1))
                dve.reciprocal(cstat[:, p, 3], cstat[:, p, 2]).then_inc(cinv_done, 1)
                dve.wait_ge(cinv_done, i * 2 + (j + 1))
                dve.tensor_tensor(cp[:, p], cp[:, p], cstat[:, p, 3].unsqueeze(2).to_broadcast([P, 4, M]), ALU.mult).then_inc(cnorm_done, 1)

            def low(i, j):
                dve.wait_ge(cp_hi, i * 2 + (j + 1))
                dve.tensor_tensor(cpT_l[:, j % 2], PS[:, 4:6], cpT_h[:, j % 2].bitcast(F32), ALU.subtract).then_inc(cp_lo, 1)

            def values(i, j):
                h, p = i + j // 2, j % 2
                dve.wait_ge(cpv_done, i * 2 + (j + 2))
                dve.tensor_scalar(qx[:, bass.ds(h * 2, 2), p * HALF:(p + 1) * HALF], PS[:, 6:8], 1.0, None, ALU.mult).then_inc(co_done, 1)

            def step(i, j):
                if in_groups(i, j):
                    largest(i, j)
                if in_groups(i, j + 1):
                    split_q(i, j + 1)
                if in_groups(i, j - 1):
                    low(i, j - 1)
                if in_groups(i, j):
                    normalise(i, j)
                if in_groups(i, j - 2):
                    values(i, j - 2)
                if j == 1 and in_groups(i, 0):
                    split_v(i, 0)

            split_q(0, 0)
            groups(dve, step)
            split_weights(0, B_O, 8, g_out)
            for k in range(KT):
                low_x(4, k, qx[:, k])
            residual(3, B_O, B_END, 8, g_out, low_gu_first)

            def to_ffn2():
                for k in range(KT):
                    low_x(5, k)

            def to_end(add_down):
                for m in range(KT):
                    add_down(PAIRS - 1, m)
                root(4)
                for k in range(KT):
                    dve.scalar_tensor_tensor(out=X[:, k], in0=X[:, k], scalar=par[:, G_FIN + k:G_FIN + k + 1], in1=RB[:],
                                             op0=ALU.mult, op1=ALU.mult).then_inc(fin_done, 1)

            ffn(1, 3, G_FFN2, to_ffn2, to_end)


def lay_out(inputs):
    a = {k: np.asarray(v) for k, v in inputs.items()}

    def tiles(v):
        return v.reshape(-1, P).T

    def blocks(w):
        return np.ascontiguousarray(w.reshape(KT, P, -1, P).transpose(2, 1, 0, 3))

    def gate_up(g, u):
        return np.ascontiguousarray(np.stack([g.reshape(KT, P, FC, P), u.reshape(KT, P, FC, P)], 3).transpose(2, 1, 0, 3, 4))

    def rows(v):
        return np.broadcast_to(v.reshape(1, -1), (P, v.size))

    par = np.concatenate([
        tiles(a["ffn1_norm_g"][0]), tiles(a["mix_norm_g"][0]), tiles(a["xattn_norm_g"][0]), tiles(a["mem_norm_g"][0]),
        tiles(a["ffn2_norm_g"][0]), tiles(a["final_norm_g"]), tiles(a["ssd_norm_g"][0]), tiles(a["diff_subln_g"][0]),
        a["conv_w"][0].reshape(5, KT, P).transpose(2, 1, 0).reshape(P, 40), tiles(a["conv_b"][0]),
        tiles(np.repeat(a["D_skip"][0], 64)),
        rows(np.concatenate([a["dt_bias_fwd"][0], a["dt_bias_bwd"][0]])),
        rows(np.concatenate([a["A_log_fwd"][0], a["A_log_bwd"][0]])),
        rows(np.concatenate([a["lambda_q1"][0], a["lambda_k1"][0], a["lambda_q2"][0], a["lambda_k2"][0]])),
    ], 1)
    assert par.shape == (P, NPAR)

    cst = np.zeros((P, NCST), np.float32)
    cst[:, IDENT:IDENT + P] = np.eye(P)
    cst[:, ONES:ONES + P] = 1
    cst[:, TRIF:TRIF + P] = np.triu(np.ones((P, P)))
    cst[:, TRIB:TRIB + P] = np.tril(np.ones((P, P)))
    cst[:, INV1024], cst[:, INV256], cst[:, INV128] = 1 / 1024, 1 / 256, 1 / 128
    inv = (1.0 / np.float32(500000.0) ** (np.arange(0, 16, 2, dtype=np.float32) / np.float32(16))).astype(np.float32)
    ang = (np.arange(S, dtype=np.float32)[:, None] * inv[None]).astype(np.float32)
    rope = np.zeros((P, 2, S), np.float32)
    rope[:, 0] = 1
    for r in range(P):
        d = r % 64
        if d < 16:
            partner = r + 8 if d < 8 else r - 8
            rope[r, 0] = np.cos(ang[:, d % 8])
            rope[r, 1] = np.sin(ang[:, d % 8]) * (-1 if d < 8 else 1)
            cst[partner, ROPEP + r] = 1
    w = a["w_in"][0]
    w_in = blocks(np.concatenate([w[:, 512:1536], w[:, 0:512], w[:, 2576:3088], w[:, 1552:2576]], 1))
    return {
        "xT": np.ascontiguousarray(a["x"][0].T.reshape(KT, P, S).transpose(1, 0, 2)),
        "memT": np.ascontiguousarray(a["mem"][0].T.reshape(KT, P, 256).transpose(1, 0, 2)),
        "par": np.ascontiguousarray(par), "cst": cst, "rope": rope,
        "wgu1": gate_up(a["ffn1_w_gate"][0], a["ffn1_w_up"][0]), "wd1": np.ascontiguousarray(a["ffn1_w_down"][0].reshape(FC, P, D)),
        "wgu2": gate_up(a["ffn2_w_gate"][0], a["ffn2_w_up"][0]), "wd2": np.ascontiguousarray(a["ffn2_w_down"][0].reshape(FC, P, D)),
        "w_in": w_in, "w_dt": np.ascontiguousarray(w[:, 1536:1552].reshape(KT, P, 16).transpose(1, 0, 2)),
        "w_out": blocks(a["w_out"][0]), "w_q": blocks(a["xattn_w_q"][0]), "w_kv": blocks(a["xattn_w_kv"][0]),
        "w_o": blocks(a["xattn_w_o"][0]),
    }


def kernel(**inputs):
    import concourse.bacc as bacc
    from concourse.bass_utils import run_bass_kernel_spmd

    nc = bacc.Bacc("TRN2", target_bir_lowering=False, num_devices=1)
    arrays = {f"in_{k}": v for k, v in lay_out(inputs).items()}
    args = [nc.dram_tensor(k, v.shape, mybir.dt.from_np(v.dtype), kind="ExternalInput").ap() for k, v in arrays.items()]
    args.append(nc.dram_tensor("out_yT", (P, KT, S), F32, kind="ExternalOutput").ap())
    build(nc, *args)
    r = run_bass_kernel_spmd(nc, [arrays], core_ids=[0])
    return r.results[0]["out_yT"].transpose(2, 1, 0).reshape(1, S, D)
```
